# Optimizing a Trainium2 kernel written in Bass

```python
import functools
import math
import jax, jax.numpy as jnp
from jax import lax
import numpy as np

D_MODEL = 2048
BATCH = 1
SEQ = 512
DEPTH = 1
DEC_BATCH = 8
DEC_SEQ = 4
PAST_LEN = 2048
PAGE_SIZE = 128

D_SSM = D_MODEL // 2
SSM_GROUP = 16
N_GROUPS = D_SSM // SSM_GROUP
SSM_STATE = 64
HEAD_DIM = 128
N_HEADS = (D_MODEL // 2) // HEAD_DIM
D_ATT = N_HEADS * HEAD_DIM
D_FF = ((8 * D_MODEL + 3 * 256 - 1) // (3 * 256)) * 256
Q_BLOCK = 128
N_IN = D_SSM + 3 * D_ATT + N_HEADS + 2 * D_MODEL
SPLIT_POINTS = [D_SSM, D_SSM + D_ATT, D_SSM + 2 * D_ATT, D_SSM + 3 * D_ATT,
                D_SSM + 3 * D_ATT + N_HEADS, D_SSM + 3 * D_ATT + N_HEADS + D_MODEL]
RMS_EPS = 1e-6
DT_MIN = 1e-3
DT_MAX = 1e-1
NEG_INF = -1e30
FGATE_BIAS_LO = 2.0
FGATE_BIAS_HI = 12.0

kernel_name = 'hybrid_s5_fox_gated_decode_step'

def rms_norm(x, g):
    xf = x.astype(jnp.float32)
    y = xf * lax.rsqrt(jnp.mean(xf * xf, axis=-1, keepdims=True) + RMS_EPS)
    return (y * g.astype(jnp.float32)).astype(x.dtype)

def project_inputs(x, norm_g, w_in, b_f, q_g, k_g):
    b, l = x.shape[0], x.shape[1]
    z = rms_norm(x, norm_g) @ w_in
    u, q, k, v, f_logit, gate_ssm, gate_att = jnp.split(z, SPLIT_POINTS, axis=-1)
    q = rms_norm(q.reshape(b, l, N_HEADS, HEAD_DIM), q_g)
    k = rms_norm(k.reshape(b, l, N_HEADS, HEAD_DIM), k_g)
    v = v.reshape(b, l, N_HEADS, HEAD_DIM)
    logf = jax.nn.log_sigmoid((f_logit + b_f).astype(jnp.float32))
    return u, q, k, v, logf, gate_ssm, gate_att

def s5_discretise(a_re, a_im, log_dt, b_re, b_im):
    a_re = a_re.astype(jnp.float32)
    a_im = a_im.astype(jnp.float32)
    dt = jnp.exp(log_dt.astype(jnp.float32))[:, None]
    mag = jnp.exp(dt * a_re)
    ang = dt * a_im
    abar_re = mag * jnp.cos(ang)
    abar_im = mag * jnp.sin(ang)
    e_re = abar_re - 1.0
    e_im = abar_im
    inv_den = 1.0 / (a_re * a_re + a_im * a_im)
    f_re = (e_re * a_re + e_im * a_im) * inv_den
    f_im = (e_im * a_re - e_re * a_im) * inv_den
    b_re = b_re.astype(jnp.float32)
    b_im = b_im.astype(jnp.float32)
    bbar_re = f_re[..., None] * b_re - f_im[..., None] * b_im
    bbar_im = f_re[..., None] * b_im + f_im[..., None] * b_re
    return abar_re, abar_im, bbar_re, bbar_im

def complex_affine_combine(e1, e2):
    a1r, a1i, b1r, b1i = e1
    a2r, a2i, b2r, b2i = e2
    return (a2r * a1r - a2i * a1i,
            a2r * a1i + a2i * a1r,
            a2r * b1r - a2i * b1i + b2r,
            a2r * b1i + a2i * b1r + b2i)

def s5_branch(u, h0_re, h0_im, a_re, a_im, log_dt, b_re, b_im, c_re, c_im, d, w_glu, b_glu):
    b, l = u.shape[0], u.shape[1]
    uf = u.astype(jnp.float32)
    abar_re, abar_im, bbar_re, bbar_im = s5_discretise(a_re, a_im, log_dt, b_re, b_im)
    ug = uf.reshape(b, l, N_GROUPS, SSM_GROUP)
    bu_re = jnp.einsum('blgc,gpc->blgp', ug, bbar_re)
    bu_im = jnp.einsum('blgc,gpc->blgp', ug, bbar_im)
    a_seq_re = jnp.broadcast_to(abar_re, (1, l, N_GROUPS, SSM_STATE))
    a_seq_im = jnp.broadcast_to(abar_im, (1, l, N_GROUPS, SSM_STATE))
    acum_re, acum_im, bcum_re, bcum_im = lax.associative_scan(
        complex_affine_combine, (a_seq_re, a_seq_im, bu_re, bu_im), axis=1)
    h0r = h0_re.astype(jnp.float32)[:, None]
    h0i = h0_im.astype(jnp.float32)[:, None]
    h_re = acum_re * h0r - acum_im * h0i + bcum_re
    h_im = acum_re * h0i + acum_im * h0r + bcum_im
    y = (jnp.einsum('blgp,gcp->blgc', h_re, c_re.astype(jnp.float32))
         - jnp.einsum('blgp,gcp->blgc', h_im, c_im.astype(jnp.float32)))
    y = y.reshape(b, l, D_SSM) + d.astype(jnp.float32) * uf
    y = jax.nn.gelu(y, approximate=False)
    y = y * jax.nn.sigmoid(y @ w_glu.astype(jnp.float32) + b_glu.astype(jnp.float32))
    return y.astype(u.dtype), h_re[:, -1], h_im[:, -1]

def fox_prompt(q, k, v, logf):
    b, l = q.shape[0], q.shape[1]
    n_blocks = l // Q_BLOCK
    scale = HEAD_DIM ** -0.5
    c_t = lax.cumsum(logf, axis=1).transpose(0, 2, 1)
    q_blocks = q.reshape(b, n_blocks, Q_BLOCK, N_HEADS, HEAD_DIM).swapaxes(0, 1)
    c_blocks = c_t.reshape(b, N_HEADS, n_blocks, Q_BLOCK).transpose(2, 0, 1, 3)
    k_pos = jnp.arange(l)

    def one_block(args):
        i, qb, cb = args
        q_pos = i * Q_BLOCK + jnp.arange(Q_BLOCK)
        s = jnp.einsum('bqhd,bkhd->bhqk', qb, k).astype(jnp.float32) * scale
        s = s + cb[..., :, None] - c_t[:, :, None, :]
        s = jnp.where(k_pos[None, :] <= q_pos[:, None], s, NEG_INF)
        p = jax.nn.softmax(s, axis=-1)
        return jnp.einsum('bhqk,bkhd->bqhd', p.astype(v.dtype), v)

    out = lax.map(one_block, (jnp.arange(n_blocks), q_blocks, c_blocks))
    return out.swapaxes(0, 1).reshape(b, l, D_ATT)

def fox_sample(q, k, v, logf, k_past, v_past, logf_past):
    b, t = q.shape[0], q.shape[1]
    n_past = k_past.shape[1]
    scale = HEAD_DIM ** -0.5
    lp = logf_past.astype(jnp.float32)
    r_past = (lax.cumsum(lp, axis=1, reverse=True) - lp).transpose(0, 2, 1)
    c_new = lax.cumsum(logf, axis=1).transpose(0, 2, 1)
    s_past = (jnp.einsum('bqhd,bkhd->bhqk', q, k_past).astype(jnp.float32) * scale
              + r_past[:, :, None, :] + c_new[:, :, :, None])
    s_new = (jnp.einsum('bqhd,bkhd->bhqk', q, k).astype(jnp.float32) * scale
             + c_new[:, :, :, None] - c_new[:, :, None, :])
    causal = jnp.tril(jnp.ones((t, t), dtype=bool))
    s_new = jnp.where(causal, s_new, NEG_INF)
    p = jax.nn.softmax(jnp.concatenate([s_past, s_new], axis=-1), axis=-1)
    out = (jnp.einsum('bhqk,bkhd->bqhd', p[..., :n_past].astype(v.dtype), v_past)
           + jnp.einsum('bhqk,bkhd->bqhd', p[..., n_past:].astype(v.dtype), v))
    return out.reshape(b, t, D_ATT)

def trunk_layer(x, h0_re, h0_im, attn_fn, norm_mix_g, w_in, b_f, q_norm_g, k_norm_g,
                ssm_a_re, ssm_a_im, ssm_log_dt, ssm_b_re, ssm_b_im, ssm_c_re, ssm_c_im, ssm_d,
                w_glu, b_glu, w_br_ssm, w_br_att, w_out, norm_ffn_g, w_ffn_gate, w_ffn_up, w_ffn_down):
    u, q, k, v, logf, gate_ssm, gate_att = project_inputs(x, norm_mix_g, w_in, b_f, q_norm_g, k_norm_g)
    y_ssm, h_re, h_im = s5_branch(u, h0_re, h0_im, ssm_a_re, ssm_a_im, ssm_log_dt, ssm_b_re, ssm_b_im,
                                  ssm_c_re, ssm_c_im, ssm_d, w_glu, b_glu)
    y_att = attn_fn(q, k, v, logf)
    merged = (jax.nn.sigmoid(gate_ssm) * (y_ssm @ w_br_ssm)
              + jax.nn.sigmoid(gate_att) * (y_att @ w_br_att))
    x = x + merged @ w_out
    xn = rms_norm(x, norm_ffn_g)
    x = x + (jax.nn.silu(xn @ w_ffn_gate) * (xn @ w_ffn_up)) @ w_ffn_down
    return x, k, v, logf, h_re, h_im

def setup_inputs(seed: int = 0) -> dict:
    key = jax.random.key(seed)
    ks = jax.random.split(key, 32)
    f32 = jnp.float32

    def nrm(k, shape, scale):
        return jax.random.normal(k, shape, f32) * scale

    n_pages = PAST_LEN // PAGE_SIZE
    n_used = DEC_BATCH * n_pages
    n_pool = n_used + max(1, n_used // 4)
    perm = jax.random.permutation(ks[0], n_pool)
    page_table = perm[:n_used].reshape(DEC_BATCH, n_pages).astype(jnp.int32)

    head_bias = jnp.linspace(FGATE_BIAS_LO, FGATE_BIAS_HI, N_HEADS, dtype=f32)
    x_prompt = nrm(ks[1], (BATCH, SEQ, D_MODEL), 1.0)
    x_sample = nrm(ks[2], (DEC_BATCH, DEC_SEQ, D_MODEL), 1.0)
    cache_k = nrm(ks[3], (DEPTH, n_pool, PAGE_SIZE, N_HEADS, HEAD_DIM), 1.0)
    cache_v = nrm(ks[4], (DEPTH, n_pool, PAGE_SIZE, N_HEADS, HEAD_DIM), 1.0)
    cache_logf = jax.nn.log_sigmoid(head_bias + nrm(ks[5], (DEPTH, n_pool, PAGE_SIZE, N_HEADS), 0.5))
    state_ssm_re = nrm(ks[6], (DEPTH, DEC_BATCH, N_GROUPS, SSM_STATE), 0.3)
    state_ssm_im = nrm(ks[7], (DEPTH, DEC_BATCH, N_GROUPS, SSM_STATE), 0.3)

    norm_mix_g = 1.0 + nrm(ks[8], (DEPTH, D_MODEL), 0.02)
    w_in = nrm(ks[9], (DEPTH, D_MODEL, N_IN), D_MODEL ** -0.5)
    b_f = head_bias[None, :] + nrm(ks[10], (DEPTH, N_HEADS), 0.1)
    q_norm_g = 1.0 + nrm(ks[11], (DEPTH, HEAD_DIM), 0.02)
    k_norm_g = 1.0 + nrm(ks[12], (DEPTH, HEAD_DIM), 0.02)
    ssm_a_re = -0.5 * jnp.exp(nrm(ks[13], (DEPTH, N_GROUPS, SSM_STATE), 0.05))
    ssm_a_im = (jnp.pi * jnp.arange(SSM_STATE, dtype=f32))[None, None, :] + nrm(ks[14], (DEPTH, N_GROUPS, SSM_STATE), 0.01)
    ssm_log_dt = jax.random.uniform(ks[15], (DEPTH, N_GROUPS), f32, math.log(DT_MIN), math.log(DT_MAX))
    ssm_b_re = nrm(ks[16], (DEPTH, N_GROUPS, SSM_STATE, SSM_GROUP), (2 * SSM_GROUP) ** -0.5)
    ssm_b_im = nrm(ks[17], (DEPTH, N_GROUPS, SSM_STATE, SSM_GROUP), (2 * SSM_GROUP) ** -0.5)
    ssm_c_re = nrm(ks[18], (DEPTH, N_GROUPS, SSM_GROUP, SSM_STATE), (2 * SSM_STATE) ** -0.5)
    ssm_c_im = nrm(ks[19], (DEPTH, N_GROUPS, SSM_GROUP, SSM_STATE), (2 * SSM_STATE) ** -0.5)
    ssm_d = nrm(ks[20], (DEPTH, D_SSM), 0.5)
    w_glu = nrm(ks[21], (DEPTH, D_SSM, D_SSM), D_SSM ** -0.5)
    b_glu = nrm(ks[22], (DEPTH, D_SSM), 0.01)
    w_br_ssm = nrm(ks[23], (DEPTH, D_SSM, D_MODEL), D_SSM ** -0.5)
    w_br_att = nrm(ks[24], (DEPTH, D_ATT, D_MODEL), D_ATT ** -0.5)
    w_out = nrm(ks[25], (DEPTH, D_MODEL, D_MODEL), D_MODEL ** -0.5)
    norm_ffn_g = 1.0 + nrm(ks[26], (DEPTH, D_MODEL), 0.02)
    w_ffn_gate = nrm(ks[27], (DEPTH, D_MODEL, D_FF), D_MODEL ** -0.5)
    w_ffn_up = nrm(ks[28], (DEPTH, D_MODEL, D_FF), D_MODEL ** -0.5)
    w_ffn_down = nrm(ks[29], (DEPTH, D_FF, D_MODEL), D_FF ** -0.5)
    return {'x_prompt': x_prompt, 'x_sample': x_sample, 'cache_k': cache_k, 'cache_v': cache_v,
            'cache_logf': cache_logf, 'state_ssm_re': state_ssm_re, 'state_ssm_im': state_ssm_im,
            'page_table': page_table, 'norm_mix_g': norm_mix_g, 'w_in': w_in, 'b_f': b_f,
            'q_norm_g': q_norm_g, 'k_norm_g': k_norm_g, 'ssm_a_re': ssm_a_re, 'ssm_a_im': ssm_a_im,
            'ssm_log_dt': ssm_log_dt, 'ssm_b_re': ssm_b_re, 'ssm_b_im': ssm_b_im, 'ssm_c_re': ssm_c_re,
            'ssm_c_im': ssm_c_im, 'ssm_d': ssm_d, 'w_glu': w_glu, 'b_glu': b_glu, 'w_br_ssm': w_br_ssm,
            'w_br_att': w_br_att, 'w_out': w_out, 'norm_ffn_g': norm_ffn_g, 'w_ffn_gate': w_ffn_gate,
            'w_ffn_up': w_ffn_up, 'w_ffn_down': w_ffn_down}

def reference(x_prompt, x_sample, cache_k, cache_v, cache_logf, state_ssm_re, state_ssm_im, page_table,
              norm_mix_g, w_in, b_f, q_norm_g, k_norm_g, ssm_a_re, ssm_a_im, ssm_log_dt, ssm_b_re, ssm_b_im,
              ssm_c_re, ssm_c_im, ssm_d, w_glu, b_glu, w_br_ssm, w_br_att, w_out, norm_ffn_g,
              w_ffn_gate, w_ffn_up, w_ffn_down):
    n_seq, n_pages = page_table.shape
    y_p, y_s = x_prompt, x_sample
    kp_l, vp_l, lfp_l, hrp_l, hip_l = [], [], [], [], []
    ks_l, vs_l, lfs_l, hrs_l, his_l = [], [], [], [], []
    for l in range(DEPTH):
        lp = (norm_mix_g[l], w_in[l], b_f[l], q_norm_g[l], k_norm_g[l], ssm_a_re[l], ssm_a_im[l],
              ssm_log_dt[l], ssm_b_re[l], ssm_b_im[l], ssm_c_re[l], ssm_c_im[l], ssm_d[l], w_glu[l],
              b_glu[l], w_br_ssm[l], w_br_att[l], w_out[l], norm_ffn_g[l], w_ffn_gate[l], w_ffn_up[l],
              w_ffn_down[l])
        h_zero = jnp.zeros((y_p.shape[0], N_GROUPS, SSM_STATE), jnp.float32)
        y_p, kp, vp, lfp, hrp, hip = trunk_layer(y_p, h_zero, h_zero, fox_prompt, *lp)
        k_past = cache_k[l][page_table].reshape(n_seq, n_pages * PAGE_SIZE, N_HEADS, HEAD_DIM)
        v_past = cache_v[l][page_table].reshape(n_seq, n_pages * PAGE_SIZE, N_HEADS, HEAD_DIM)
        lf_past = cache_logf[l][page_table].reshape(n_seq, n_pages * PAGE_SIZE, N_HEADS)
        attn_sample = functools.partial(fox_sample, k_past=k_past, v_past=v_past, logf_past=lf_past)
        y_s, ksn, vsn, lfs, hrs, his = trunk_layer(y_s, state_ssm_re[l], state_ssm_im[l], attn_sample, *lp)
        kp_l.append(kp); vp_l.append(vp); lfp_l.append(lfp); hrp_l.append(hrp); hip_l.append(hip)
        ks_l.append(ksn); vs_l.append(vsn); lfs_l.append(lfs); hrs_l.append(hrs); his_l.append(his)
    new_k_prompt = jnp.stack(kp_l)
    new_v_prompt = jnp.stack(vp_l)
    new_logf_prompt = jnp.stack(lfp_l)
    new_ssm_re_prompt = jnp.stack(hrp_l)
    new_ssm_im_prompt = jnp.stack(hip_l)
    new_k_sample = jnp.stack(ks_l)
    new_v_sample = jnp.stack(vs_l)
    new_logf_sample = jnp.stack(lfs_l)
    new_ssm_re_sample = jnp.stack(hrs_l)
    new_ssm_im_sample = jnp.stack(his_l)
    return (y_p, y_s, new_k_prompt, new_v_prompt, new_logf_prompt, new_ssm_re_prompt, new_ssm_im_prompt,
            new_k_sample, new_v_sample, new_logf_sample, new_ssm_re_sample, new_ssm_im_sample)


_drawn_inputs = setup_inputs


def setup_inputs(seed=0):
    import zlib

    import numpy as np

    out = dict(_drawn_inputs(seed))
    spreads = {}
    factors = {'norm_mix_g': 2.85,
     'q_norm_g': 8.0,
     'k_norm_g': 3.059,
     'w_glu': 3.164,
     'b_glu': 64.0,
     'norm_ffn_g': 3.891}
    for name, (base, spread) in spreads.items():
        noise = np.random.default_rng([zlib.crc32(name.encode()), seed]).standard_normal(out[name].shape)
        drawn = base * np.exp(spread * noise) if base else spread * noise
        out[name] = __import__('jax').numpy.asarray(drawn.astype(out[name].dtype))
    for name, factor in factors.items():
        out[name] = (out[name] * factor).astype(out[name].dtype)
    return out
```

```python
import math

import concourse.bass as bass
from concourse import mybir

F32 = mybir.dt.float32
F32R = mybir.dt.float32r
I32 = mybir.dt.int32
ALU = mybir.AluOpType
ACT = mybir.ActivationFunctionType
AX_X = mybir.AxisListType.X

P = 128
D_MODEL, SEQ, DEC_BATCH, DEC_SEQ = 2048, 512, 8, 4
PAGE, N_PAGES = 128, 16
HEADS = 8
D_SSM = D_MODEL // 2
D_FF = 5632
NS = DEC_BATCH * DEC_SEQ
T = SEQ + NS
HT = T // 2
KD = D_MODEL // P
KH = D_SSM // P
STILES = 32
LEVELS = 9
SCALE = P ** -0.5
EPS = 1e-6
NEG = -1e30
TWO_PI = 2 * math.pi
MAGIC = 1.5 * 2.0 ** 23
COL_F = D_SSM + 3 * D_SSM
COL_GS = COL_F + HEADS
COL_GA = COL_GS + D_MODEL
KU = 8
RAW, SPLIT = 4, 2
FF_BLOCKS, FF_TILES = 4, 11
ALL = slice(None)


def two_pi_parts():
    import numpy as np

    parts, rest = [], TWO_PI
    for bits in (8, 12):
        e = math.floor(math.log2(abs(rest))) - bits
        part = math.floor(rest / 2.0 ** e) * 2.0 ** e
        parts.append(part)
        rest -= part
    return parts + [float(np.float32(rest))]


def build(nc, x_prompt, x_sample, cache_k, cache_v, cache_logf, state_re, state_im, page_table,
          norm_mix_g, w_in, b_f, q_norm_g, k_norm_g, a_re, a_im, log_dt, b_re, b_im, c_re, c_im, ssm_d,
          w_glu, b_glu, w_br_ssm, w_br_att, w_out, norm_ffn_g, w_gate, w_up, w_down,
          y_prompt, y_sample, nk_p, nv_p, nlf_p, sre_p, sim_p, nk_s, nv_s, nlf_s, sre_s, sim_s):
    base = 16512
    tile_b = T * 4
    t8 = 8 * tile_b

    def at(name, shape, dt, off):
        return nc.alloc_sbuf_tensor_at(name, shape, dt, offset=base + off)

    o_xh, o_xl, o_u = 0, 2 * t8, 4 * t8
    o_q, o_k, o_v, o_c = 5 * t8, 6 * t8, 7 * t8, 8 * t8
    o_raw = 10 * t8
    o_sh = o_raw + RAW * 4096
    o_sl = o_sh + SPLIT * 4096
    o_misc = o_sl + SPLIT * 4096
    xn_hi = at("xn_hi", [P, KD, T], F32R, o_xh)
    xn_lo = at("xn_lo", [P, KD, T], F32R, o_xl)
    x_t = at("x_t", [P, KD, T], F32, o_u)
    u = at("u", [P, KH, T], F32, o_u)
    q = at("q", [P, KH, T], F32, o_q)
    k = at("k", [P, KH, T], F32, o_k)
    v = at("v", [P, KH, T], F32, o_v)
    raw = at("raw", [P, RAW, KU, P], F32, o_raw)
    w_hi = at("w_hi", [P, SPLIT, KU, P], F32R, o_sh)
    w_lo = at("w_lo", [P, SPLIT, KU, P], F32R, o_sl)
    m = [o_misc]

    def small(name, shape, dt=F32):
        n = 4
        for d in shape[1:]:
            n *= d
        off = m[0]
        m[0] += (n + 31) // 32 * 32
        assert m[0] <= 229344 - base, (name, m[0] - 229344 + base)
        return at(name, shape, dt, off)

    ident = small("ident", [P, P])
    ones = small("ones", [P, P])
    vecs = small("vecs", [P, 50])
    consts = small("consts", [P, 4])
    V_MIX, V_FFN, V_D, V_BGLU, V_QG, V_KG = 0, 16, 32, 40, 48, 49
    bf_col = small("bf_col", [HEADS, 1])
    pages = small("pages", [1, DEC_BATCH * N_PAGES], I32)
    use_c = small("use_c", [P, 2, P])
    lf_nat = small("lf_nat", [P, 5, 2, HEADS])
    cum = small("cum", [HEADS, T])

    cm = [o_c]

    def in_c(name, shape, dt=F32):
        n = 4
        for d in shape[1:]:
            n *= d
        off = cm[0]
        cm[0] += (n + 31) // 32 * 32
        assert cm[0] <= o_raw, name
        return at(name, shape, dt, off)

    tab_b = in_c("tab_b", [P, KH, 2, P])
    tab_c = in_c("tab_c", [P, KH, 2, P])
    o_scan = cm[0]
    h_both = in_c("h_both", [P, 2, 2, T])
    h_re, h_im = h_both[:, 0, :, :], h_both[:, 1, :, :]
    use_b = in_c("use_b", [P, 2, P])
    use_u = in_c("use_u", [P, T])
    pow_a = in_c("pow_a", [P, LEVELS, 3, STILES])
    use_p = in_c("use_p", [P, LEVELS, 3, 4])
    st_s = in_c("st_s", [P, 2, DEC_BATCH, STILES])
    st_w = in_c("st_w", [P, 2, DEC_BATCH])
    prods = in_c("prods", [P, 2, 2, DEC_BATCH])
    st_p = in_c("st_p", [P, 2, STILES])

    ps = nc.alloc_psum_tensor("ps", [P, 8, 512], F32)

    def sem(name):
        return nc.alloc_semaphore(name)

    class Ring:
        n = RAW
        loads = [0] * RAW

    s_passed = {n: sem(f"passed_{n}") for n in ("sp", "pool", "act", "dve")}

    def settle(eng, name):
        eng.sem_inc(s_passed[name], 1)

    s_landed = [sem(f"weights_landed{i}") for i in range(RAW)]
    s_hi = sem("weights_hi")
    s_lo = sem("weights_lo")
    s_used = sem("weights_used")

    class Phase:

        def __init__(self, per, times, first=None, base=None):
            self.per, self.skip, self.times = per, -per % RAW, times
            self.loads = [len(range(s, per, RAW)) for s in range(RAW)]
            self.first, self.base = first, base
            if base is None:
                self.first, self.base = Ring.n, list(Ring.loads)
                Ring.n += (per + self.skip) * times
                Ring.loads = [b + l * times for b, l in zip(self.base, self.loads)]

        @staticmethod
        def repeat(phases, times):
            units = Ring.n - phases[0].first
            Ring.n += units * (times - 1)
            Ring.loads = [b + units // RAW * (times - 1) for b in Ring.loads]
            for p in phases:
                p.block_units = units

        def in_block(self, n):
            return Phase(self.per, self.times, n * self.block_units + self.first,
                         [n * (self.block_units // RAW) + b for b in self.base])

        def of(self, i, j):
            return i * (self.per + self.skip) + (self.first + j)

        def used(self, i, j):
            return self.of(i, j) + 1

        def landed(self, i, j):
            s = j % RAW
            return s_landed[s], i * (16 * self.loads[s]) + (self.base[s] + (j // RAW + 1)) * 16

        def inc(self, j):
            return 1 + (self.skip if j == self.per - 1 else 0)

        def load(self, eng, i, j, parts):
            eng.wait_ge(s_hi, self.of(i, j) - (RAW - 1))
            eng.wait_ge(s_lo, self.of(i, j) - (RAW - 1))
            settle(eng, "sp")
            eng.dma_start(raw[:, j % RAW, 0:parts.shape[1], :], parts).then_inc(s_landed[j % RAW], 16)

        def slot_used(self, i, j):
            return self.of(i, self.per - 1) if j == self.per else self.of(i, j) - (SPLIT - 1)

        def split_hi(self, eng, i, j, n=KU):
            s, value = self.landed(i + j // self.per, j % self.per)
            eng.wait_ge(s, value)
            eng.wait_ge(s_used, self.slot_used(i, j))
            j %= self.per
            eng.activation(w_hi[:, j % SPLIT, 0:n, :], raw[:, j % RAW, 0:n, :], ACT.Copy)\
               .then_inc(s_hi, self.inc(j))

        def split_lo(self, eng, i, j, n=KU):
            eng.wait_ge(s_hi, self.of(i + j // self.per, j % self.per) + 1)
            eng.wait_ge(s_used, self.slot_used(i, j))
            j %= self.per
            eng.tensor_tensor(w_lo[:, j % SPLIT, 0:n, :], raw[:, j % RAW, 0:n, :],
                              w_hi[:, j % SPLIT, 0:n, :].bitcast(F32), ALU.subtract)\
               .then_inc(s_lo, self.inc(j))

        def product(self, eng, i, j, pair, hi, lo, first, last, n=KU, tiles=None, wait=True, done=True):
            if wait:
                eng.wait_ge(s_lo, self.of(i, j) + 1)
            s = j % SPLIT
            tiles = range(n) if tiles is None else tiles
            for kt in tiles:
                for w, x in ((w_hi, hi), (w_hi, lo), (w_lo, hi)):
                    for half in range(2):
                        mm = eng.matmul(ps[:, 2 * pair + half, 0:HT], w[:, s, kt, :], x(kt, half),
                                        start=first and kt == 0 and w is w_hi and x is hi,
                                        stop=last and kt == n - 1 and w is w_lo)
            if done:
                mm.then_inc(s_used, self.inc(j))
            return mm

    def halves(t, tile):
        return lambda kt, half: t[:, tile(kt), half * HT:(half + 1) * HT]

    def w_cols(w, k0, nk, c0, n=P):
        return w[0, k0 * P:(k0 + nk) * P, bass.ds(c0, n)].rearrange("(t p) n -> p t n", p=P)

    def w_rows(w, k0, nk, c0):
        return w[0, bass.ds(k0, nk * P), bass.ds(c0, P)].rearrange("(t p) n -> p t n", p=P)

    ph_f = Phase(2, 1)
    ph_u = Phase(4, 4)
    ph_qkv = Phase(6, HEADS)
    ph_glu = Phase(4, 2)
    ph_merge = Phase(6, KD)
    ph_out = Phase(4, 8)
    ph_ffn = Phase(4, FF_TILES), Phase(4, KD // 2)
    Phase.repeat(ph_ffn, FF_BLOCKS)
    ph_end = Phase(1, 1)

    PHASES = ("setup", "normed", "u", "qkv", "states", "prompt", "sample", "merged", "out", "ffn_normed", "ffn")
    s_all = sem("all_at_barrier")

    def reached(name):
        return 4 * (PHASES.index(name) + 1)

    def barrier(eng, name):
        eng.drain().then_inc(s_all, 1)
        eng.wait_ge(s_all, reached(name))

    class Chain:

        def __init__(self, name):
            self.sem, self.n = sem(name), 0

        def __call__(self, eng, ins):
            self.n += 1
            ins.then_inc(self.sem, 1)
            eng.wait_ge(self.sem, self.n)

    o = [o_k]

    def tmp(name, shape, dt=F32):
        n = 4
        for d in shape[1:]:
            n *= d
        off = o[0]
        o[0] += (n + 31) // 32 * 32
        assert o[0] <= o_c, name
        return at(name, shape, dt, off)

    rows = tmp("rows", [50, P])
    nat = tmp("nat", [STILES, 24, P])
    dt2 = tmp("dt2", [STILES, 2])
    dt_w = tmp("dt_w", [STILES, 2, 2])
    dt_i = tmp("dt_i", [STILES, 2], I32)
    nat_i = tmp("nat_i", [STILES, P], I32)
    o_b = o[0]
    b_nat = tmp("b_nat", [P, 2, STILES, 16])
    b_tmp = tmp("b_tmp", [P, 2, STILES, 16])
    b_pad = tmp("b_pad", [P, 2, KH, 4, 2, 16])
    f_col = tmp("f_col", [P, 2, STILES])
    h0_nat = tmp("h0_nat", [P, 2, 2, P])
    par_i = tmp("par_i", [P, 2], I32)
    c_nat = at("c_nat", [P, 2, KH, 64], F32, o_q + 5 * tile_b)
    c_pad = at("c_pad", [P, 2, KH, 2, 64], F32, o_b)
    (N_DT, N_ARE, N_AIM, N_MAG, N_ANG, N_K, N_R, N_SIN, N_COS, N_ABS, N_ER, N_T1, N_T2, N_DEN, N_INV,
     N_ABR, N_ABI, N_FR, N_FI) = range(19)
    nt = lambda i: nat[:, i, :]

    x_nat = at("x_nat", [P, 2, D_MODEL], F32, o_xh)
    x_smp = at("x_smp", [NS, D_MODEL], F32, o_xl)
    sq = at("sq", [P, 2, T], F32, o_scan)
    scaled = at("scaled", [P, 2, T], F32, o_scan + 2 * tile_b)
    rstd = at("rstd", [P, T], F32, o_scan + 4 * tile_b + 1024)

    s_small = sem("small_inputs")
    s_dt = sem("discretisation_inputs")
    s_vec = sem("vectors_landed")
    s_x = [sem("x_landed0"), sem("x_landed1")]
    s_xs = sem("x_sample_landed")
    s_xt = sem("x_transposed")
    s_xc = sem("x_copied")
    s_ident = sem("ident_ready")
    dve = Chain("dve_steps")
    s_setup_t = sem("setup_transposed")
    s_setup_c = sem("setup_copied")
    s_exp = sem("setup_act")
    s_dve_s = sem("setup_dve")
    lf_w = at("lf_w", [HEADS, 4, T], F32, o_q)
    lf_i = at("lf_i", [HEADS, T], I32, o_q + 4 * tile_b)
    s_fm, s_lf, s_lft = sem("f_product"), sem("logf_steps"), sem("logf_turned")
    s_uev, s_cn = [sem("u_copied0"), sem("u_copied1")], sem("c_landed")

    s_m = sem("qkv_product")
    s_ev = sem("qkv_copied")
    s_bu = sem("bu_product")
    s_buc = sem("bu_copied")
    s_qsum, s_qrs, s_qn = sem("qk_sum"), sem("qk_root"), sem("qk_normed")
    s_h, s_ch, s_yev = sem("states_scanned"), sem("states_used"), sem("y_copied")
    s_pw = sem("qk_rstd")
    s_scan = sem("scan_steps")
    s_up = sem("use_p_ready")
    s_steps, s_hs = sem("sample_steps"), sem("sample_states_ready")
    s_ub, s_uc = sem("use_b_ready"), sem("use_c_ready")
    A, B, C, D = range(4)

    def pair(n):
        return ps[:, 2 * n:2 * n + 2, 0:HT]

    def two(ap):
        return ap.rearrange("p (a n) -> p a n", a=2)

    def tile_of(t, i):
        return t[:, bass.ds(i, 1), :].rearrange("p a n -> p (a n)")

    norm_sems = {name: {x: sem(f"norm_{name}_{x}") for x in
                        ("squares", "summed", "root", "rstd", "scaled", "hi", "lo", "lo_odd")}
                 for name in ("mix", "ffn")}
    norm_gain = {"mix": 0, "ffn": 16}

    def norm_act(act, name):
        s = norm_sems[name]
        for t in range(KD):
            if t >= 2:
                act.wait_ge(s["summed"], t - 1)
            act.activation(sq[:, t % 2, :], x_t[:, t, :], ACT.Square).then_inc(s["squares"], 1)
        act.wait_ge(s["summed"], KD)
        act.activation(two(rstd[:, :]), pair(D), ACT.Sqrt, scale=1.0 / D_MODEL, bias=consts[:, 1:2])
        act.activation(two(scaled[:, 0, :]), pair(D), ACT.Identity, scale=1.0 / D_MODEL, bias=consts[:, 1:2])\
           .then_inc(s["root"], 1)
        for t in range(KD):
            act.wait_ge(s["scaled"], t + 1)
            act.activation(xn_hi[:, t, :], scaled[:, t % 2, :], ACT.Copy).then_inc(s["hi"], 1)

    def norm_pe(pe, name):
        s = norm_sems[name]
        for t in range(KD):
            pe.wait_ge(s["squares"], t + 1)
            for half in range(2):
                mm = pe.matmul(ps[:, 2 * D + half, 0:HT], ones[:, :], sq[:, t % 2, half * HT:(half + 1) * HT],
                               start=t == 0, stop=t == KD - 1)
            mm.then_inc(s["summed"], 1)

    def normed_tiles(pe, name, n):
        pe.wait_ge(norm_sems[name]["lo"], n // 2)
        pe.wait_ge(norm_sems[name]["lo_odd"], n // 2)

    def norm_dve(eng, name):
        s = norm_sems[name]
        eng.wait_ge(s["root"], 1)
        eng.reciprocal(rstd[:, :], rstd[:, :]).then_inc(s["rstd"], 1)
        r, x, w = rstd[:, :], scaled[:, 0, :], scaled[:, 1, :]
        eng.wait_ge(s["rstd"], 1)
        eng.scalar_tensor_tensor(w, r, -0.5, r, ALU.mult, ALU.mult).then_inc(s["rstd"], 1)
        eng.wait_ge(s["rstd"], 2)
        eng.tensor_tensor(w, w, x, ALU.mult).then_inc(s["rstd"], 1)
        eng.wait_ge(s["rstd"], 3)
        eng.scalar_tensor_tensor(r, w, 1.5, r, ALU.add, ALU.mult).then_inc(s["rstd"], 1)
        eng.wait_ge(s["rstd"], 4)
        def odd_lo(t):
            eng.wait_ge(s["hi"], t + 1)
            eng.tensor_tensor(xn_lo[:, t, :], scaled[:, 1, :], xn_hi[:, t, :].bitcast(F32), ALU.subtract)\
               .then_inc(s["lo_odd"], 1)

        for t in range(KD):
            if t >= 3 and t % 2:
                odd_lo(t - 2)
                eng.wait_ge(s["lo_odd"], (t - 1) // 2)
            elif t >= 2 and t % 2 == 0:
                eng.wait_ge(s["lo"], t // 2)
            g = norm_gain[name] + t
            eng.scalar_tensor_tensor(scaled[:, t % 2, :], x_t[:, t, :], vecs[:, g:g + 1], rstd[:, :],
                                     ALU.mult, ALU.mult).then_inc(s["scaled"], 1)
        odd_lo(KD - 1)

    def norm_pool(pool, name):
        s = norm_sems[name]
        for t in range(0, KD, 2):
            pool.wait_ge(s["hi"], t + 1)
            pool.tensor_tensor(xn_lo[:, t, :], scaled[:, t % 2, :], xn_hi[:, t, :].bitcast(F32),
                               ALU.subtract).then_inc(s["lo"], 1)

    cp = [o_c]

    def in_p(name, shape, dt=F32, limit=o_raw):
        n = 4
        for d in shape[1:]:
            n *= d
        off = cp[0]
        cp[0] += (n + 31) // 32 * 32
        assert cp[0] <= limit, (name, cp[0] - limit)
        return at(name, shape, dt, off)

    QB = SEQ // P
    ORDER = tuple(range(QB - 1, -1, -1))
    off = [i * (i + 1) // 2 * P for i in range(QB + 1)]
    poff = [0, 4 * P, 7 * P, 9 * P, 10 * P]
    stage = in_p("stage", [P, 2, 3, T])
    nat_kv = in_p("nat_kv", [P, 2, QB, P])
    nat_s = in_p("nat_s", [NS, 2, P])
    prob = in_p("prob", [P, off[QB]])
    prob_t = in_p("prob_t", [P, poff[QB]])
    cm = in_p("cm", [HEADS, T])
    causal = in_p("causal", [P, P])
    stat = in_p("stat", [P, 3, QB])
    vs_nat = at("vs_nat", [NS, HEADS, P], F32, o_sl + 4096)
    st_out = at("st_out", [P, 2, 2, P], F32, o_sh + 4096)
    stp_out = at("stp_out", [STILES, 2, P], F32, o_sh + 4096 + 2048)
    s_st, s_stc, s_store = sem("states_turned"), sem("states_copied"), sem("stored")
    s_causal = sem("causal_ready")
    s_stage, s_cm, s_cb, s_bias, s_bm = sem("staged"), sem("cm_ready"), sem("c_spread"), sem("bias_copied"), sem("bias_masked")
    s_qk, s_kv, s_kvc, s_kst = sem("qk_product"), sem("kv_turned"), sem("kv_copied"), sem("kv_stored")
    s_sc, s_nm, s_ex, s_pr = sem("scored"), sem("max_ready"), sem("exp_ready"), sem("prob_ready")
    s_pt, s_ptc, s_pv, s_oc = sem("prob_turned"), sem("prob_copied"), sem("pv_product"), sem("out_copied")
    s_mx, s_rs2 = sem("max_steps"), sem("rsum_steps")

    GH = 4
    PG = 8
    GROUPS = N_PAGES // 4
    ROUNDS = N_PAGES + GROUPS
    scores = at("scores", [P, 2, N_PAGES * PAGE], F32, o_k)
    o_rows = at("o_rows", [P, 2, P], F32, o_k + 16384)
    page = at("page", [P, PG, HEADS * P], F32, o_v)
    key_t = at("key_t", [P, 2, 2, GH * PAGE], F32, o_v + PG * 4096)
    zeros = at("zeros", [P, 2 * P], F32, o_v + PG * 4096 + 8192)
    o_small = [o_v + PG * 4096 + 16384]

    def in_s(name, shape, dt=F32, start=None, limit=o_raw + 4096):
        if start is not None:
            o_small[0] = start
        n = 4
        for d in shape[1:]:
            n *= d
        a = at(name, shape, dt, o_small[0])
        o_small[0] += (n + 31) // 32 * 32
        assert o_small[0] <= limit, name
        return a

    qs = in_s("qs", [P, HEADS, NS])
    ks = in_s("ks", [P, HEADS, NS])
    new_sc = in_s("new_sc", [P, 2, NS])
    new_ex = in_s("new_ex", [P, 2, NS])
    new_pr = in_s("new_pr", [P, 2, NS], limit=o_raw)
    sel = in_s("sel", [P, 2, GH, NS], start=o_raw)
    sel_c = in_s("sel_c", [HEADS, 2, GH, NS])
    rep = in_s("rep", [NS, GH, NS])
    mask32 = in_s("mask32", [NS, NS + DEC_BATCH])
    neg_c = in_s("neg_c", [HEADS, NS])
    mask = in_s("mask", [P, NS + DEC_BATCH])
    c_query, s_max, s_nmax, s_tot, s_rec1 = (
        in_s(n, [P, 2]) for n in ("c_query", "s_max", "s_nmax", "s_tot", "s_rec1"))
    run_max = in_s("run_max", [P, 2, GROUPS + 1])
    exp_part = in_s("exp_part", [P, 2, GROUPS + 1])
    part_sum = in_s("part_sum", [P, 2])
    head_of = in_s("head_of", [P, HEADS])
    page_of = in_s("page_of", [P, N_PAGES])
    decay_p = at("decay_p", [P, 4, 2, PAGE], F32, o_sh + 4096)
    new_pt = at("new_pt", [NS, 2, P], F32, o_raw + 1024)
    lf_rows = at("lf_rows", [DEC_BATCH * N_PAGES, PAGE, HEADS], F32, o_raw + 4096)
    lf_past = at("lf_past", [PAGE, DEC_BATCH, N_PAGES, HEADS], F32, o_raw + 8192)
    lf_later = at("lf_later", [PAGE, DEC_BATCH, N_PAGES, HEADS], F32, o_raw + 4096)
    prob_st = at("prob_st", [P, 2, 2, 4 * PAGE], F32, o_raw + 4096)
    decay = at("decay", [P, DEC_BATCH, PAGE], F32, o_raw + 12288)
    later = at("later", [PAGE, PAGE], F32, o_v + PG * 4096)
    s_lfp, s_pool_c, s_sp = sem("past_logf_landed"), sem("sample_constants"), sem("sample_prep")
    s_spe, s_spc = sem("sample_prep_product"), sem("sample_prep_copied")
    s_dp = sem("decay_spread")
    s_page = [sem(f"page_landed{i}") for i in range(PG)]
    s_tt, s_tca, s_tcd = sem("turned"), sem("turned_copied_act"), sem("turned_copied_dve")
    s_sco, s_ta, s_td = sem("page_scored"), sem("scores_copied_act"), sem("scores_copied_dve")
    s_sm, s_sx, s_pvp, s_lft2 = sem("softmax_steps"), sem("sample_exp"), sem("page_summed"), sem("past_logf_turned")
    s_fin, s_finc = sem("sample_end_product"), sem("sample_end_copied")

    y1_hi, y1_lo = (at(n, [P, KH, T], F32R, o) for n, o in (("y1_hi", o_k), ("y1_lo", o_v)))
    glu_gate = at("glu_gate", [P, 2, T], F32, o_c)
    ys_hi, ys_lo = (at(n, [P, KH, T], F32R, o) for n, o in (("ys_hi", o_k), ("ys_lo", o_u)))
    ya_hi, ya_lo = (at(n, [P, KH, T], F32R, o) for n, o in (("ya_hi", o_v), ("ya_lo", o_q)))
    merged = at("merged", [P, KD, T], F32, o_c)
    att_gate = at("att_gate", [P, T], F32, m[0] - tile_b)
    x_again = at("x_again", [P, 2, D_MODEL], F32, o_k)
    x_smp2 = at("x_smp2", [NS, D_MODEL], F32, o_v)
    hid_hi = at("hid_hi", [P, FF_TILES, T], F32R, o_k)
    hid_lo = at("hid_lo", [P, FF_TILES, T], F32R, o_k + FF_TILES * tile_b)
    ff_act = at("ff_act", [P, T], F32, o_k + 2 * FF_TILES * tile_b)
    hid = at("hid", [P, T], F32, o_k + (2 * FF_TILES + 1) * tile_b)
    y_nat = at("y_nat", [P, 2, D_MODEL], F32, o_k)
    s_gelu, s_y1h, s_y1l, s_y1l2, s_gg, s_ys = sem("gelu_ready"), sem("y1_hi_ready"), sem("y1_lo_even"), sem("y1_lo_odd"), sem("glu_gate_ready"), sem("y_ssm_ready")
    s_ysh, s_ysl, s_yah, s_yal = sem("y_ssm_hi_ready"), sem("y_ssm_lo_ready"), sem("y_att_hi_ready"), sem("y_att_lo_ready")
    s_gs, s_ga, s_mg = sem("ssm_gate_ready"), sem("att_gate_ready"), sem("merge_steps")
    s_mhi, s_mhi2, s_mlo, s_mlo2 = sem("merged_hi_act"), sem("merged_hi_dve"), sem("merged_lo_pool"), sem("merged_lo_dve")
    s_x2 = [sem("x_again_landed0"), sem("x_again_landed1")]
    s_xs2, s_x2t, s_x2c = sem("x_sample_again"), sem("x_again_turned"), sem("x_again_copied")
    s_res = [sem("residual_added0"), sem("residual_added1")]
    s_silu, s_hid, s_hh, s_hl = sem("silu_ready"), sem("hidden_ready"), sem("hidden_hi"), sem("hidden_lo")
    s_dn = [sem("down_added0"), sem("down_added1")]
    s_yt, s_yca, s_ycd, s_yst = sem("y_turned"), sem("y_rows_act"), sem("y_rows_dve"), [sem("y_stored0"), sem("y_stored1")]
    FF_UNITS = ((0, 6), (6, 5))
    FF_SPLIT = (KU, 5, 6, 5, KU)

    with nc.Block() as block:

        @block.sync
        def _(sp):
            sp.dma_start(rows[0:16, :], norm_mix_g.rearrange("a (t p) -> (a t) p", p=P)).then_inc(s_vec, 16)
            sp.dma_start(rows[16:32, :], norm_ffn_g.rearrange("a (t p) -> (a t) p", p=P)).then_inc(s_vec, 16)
            sp.dma_start(rows[32:40, :], ssm_d.rearrange("a (t p) -> (a t) p", p=P)).then_inc(s_vec, 16)
            sp.dma_start(rows[40:48, :], b_glu.rearrange("a (t p) -> (a t) p", p=P)).then_inc(s_vec, 16)
            sp.dma_start(rows[48:49, :], q_norm_g).then_inc(s_vec, 16)
            sp.dma_start(rows[49:50, :], k_norm_g).then_inc(s_vec, 16)
            for t in range(2):
                sp.dma_start(x_nat[:, t, :], x_prompt[0, t * P:(t + 1) * P, :]).then_inc(s_x[t], 16)
            sp.dma_start(x_smp[:, :], x_sample.rearrange("b s d -> (b s) d")).then_inc(s_xs, 16)
            sp.dma_start(nt(N_ARE), a_re[0].rearrange("(s g) p -> s (g p)", g=2)).then_inc(s_dt, 16)
            sp.dma_start(nt(N_AIM), a_im[0].rearrange("(s g) p -> s (g p)", g=2)).then_inc(s_dt, 16)
            sp.dma_start(dt2[:, :], log_dt[0].rearrange("(s g) -> s g", g=2)).then_inc(s_dt, 16)
            for c, w in enumerate((b_re, b_im)):
                sp.dma_start(b_nat[:, c, :, :], w[0].rearrange("(s g) p c -> (g p) s c", g=2))\
                  .then_inc(s_small, 16)
            for c, w in enumerate((state_re, state_im)):
                sp.dma_start(h0_nat[:, c, :, :],
                             w[0].rearrange("(a b) (s g) p -> (b s) a (g p)", a=2, g=2)).then_inc(s_small, 16)
            sp.dma_start(bf_col[:, :], b_f.rearrange("a h -> h a")).then_inc(s_small, 16)
            sp.dma_start(pages[:, :], page_table.rearrange("(o b) n -> o (b n)", o=1)).then_inc(s_small, 16)
            for t in range(2):
                sp.wait_ge(s_xt, 4 * (t + 1))
                sp.dma_start(x_nat[:, t, :], x_prompt[0, (t + 2) * P:(t + 3) * P, :]).then_inc(s_x[t], 16)
            for j in range(2):
                ph_f.load(sp, 0, j, w_cols(w_in, KU * j, KU, COL_F))
            sp.wait_ge(s_all, reached("normed"))
            for c, w in enumerate((c_re, c_im)):
                sp.dma_start(c_nat[:, c, :, :], w[0].rearrange("(t g) c p -> (g c) t p", t=KH))\
                  .then_inc(s_cn, 16)
            with sp.Fori(0, ph_u.times) as i:
                for j in range(4):
                    ph_u.load(sp, i, j, w_cols(w_in, KU * (j % 2), KU, i * (2 * P) + (j // 2) * P))
            with sp.Fori(0, HEADS) as i:
                for j in range(6):
                    ph_qkv.load(sp, i, j, w_cols(w_in, KU * (j % 2), KU, i * P + (1 + j // 2) * D_SSM))
            ph_glu.load(sp, 0, 0, w_cols(w_glu, 0, KU, 0))
            sp.wait_ge(s_stc, 1)
            for c, (big, one) in enumerate(((sre_s, sre_p), (sim_s, sim_p))):
                sp.dma_start(big[0].rearrange("(a b) (s g) p -> (b s) a (g p)", a=2, g=2), st_out[:, c, :, :])\
                  .then_inc(s_store, 16)
                sp.dma_start(one[0, 0].rearrange("(s g) p -> s (g p)", g=2), stp_out[:, c, :]).then_inc(s_store, 16)
            sp.dma_start(nlf_p[0, 0].rearrange("(a p) h -> p a h", p=P), lf_nat[:, 0:4, 0, :]).then_inc(s_store, 16)
            sp.dma_start(nlf_s[0].rearrange("b s h -> (b s) h"), lf_nat[0:NS, 4, 0, :]).then_inc(s_store, 16)
            for h in range(HEADS):
                sp.wait_ge(s_kvc, h + 2)
                for c, (big, small_) in enumerate(((nk_p, nk_s), (nv_p, nv_s))):
                    sp.dma_start(big[0, 0, :, bass.ds(h, 1), :].rearrange("(a p) h d -> p a (h d)", p=P),
                                 nat_kv[:, c, :, :]).then_inc(s_kst, 16)
                    sp.dma_start(small_[0, :, :, bass.ds(h, 1), :].rearrange("b s h d -> (b s) (h d)"),
                                 nat_s[:, c, :]).then_inc(s_kst, 16)
                for p in range(N_PAGES):
                    idx = sp.value_load(pages[0:1, bass.ds(h * N_PAGES + p, 1)], min_val=0,
                                        max_val=cache_k.shape[1] - 1)
                    sp.dma_start(lf_rows[h * N_PAGES + p:h * N_PAGES + p + 1, :, :].rearrange("r k h -> r (k h)"),
                                 cache_logf[0, bass.ds(idx, 1), :, :].rearrange("a k h -> a (k h)"))\
                      .then_inc(s_lfp, 16)
            sp.wait_ge(s_kst, 64 * HEADS + 1)
            sp.wait_ge(s_store, 16 * 6)
            sp.wait_ge(s_all, reached("prompt"))
            with sp.Fori(0, DEC_BATCH) as b:
                for c, cache in enumerate((cache_k, cache_v)):
                    for p in range(N_PAGES):
                        idx = sp.value_load(pages[0:1, bass.ds(b * N_PAGES + p, 1)], min_val=0,
                                            max_val=cache_k.shape[1] - 1)
                        if c == 0 and p < PG:
                            sp.wait_ge(s_pvp, b * N_PAGES + (p + PG + 1 + 1))
                        elif c == 0:
                            sp.wait_ge(s_tt, b * ROUNDS + (p - PG + 1 + 1))
                        elif p < PG:
                            sp.wait_ge(s_tt, b * ROUNDS + (p + PG + 1 + 1))
                        else:
                            sp.wait_ge(s_pvp, b * N_PAGES + (N_PAGES + p - PG + 1 + 1))
                        sp.dma_start(page[:, p % PG, :],
                                     cache[0, bass.ds(idx, 1), :, :, :].rearrange("a p h d -> p (a h d)"))\
                          .then_inc(s_page[p % PG], 16)
            sp.wait_ge(s_all, reached("sample"))
            for j in range(1, 4):
                ph_glu.load(sp, 0, j, w_cols(w_glu, 0, KU, j * P))
            for j in range(4):
                ph_glu.load(sp, 1, j, w_cols(w_glu, 0, KU, (4 + j) * P))
            with sp.Fori(0, KD) as i:
                for j in range(4):
                    ph_merge.load(sp, i, j, w_cols(w_in, KU * (j % 2), KU, i * P + (COL_GS if j < 2 else COL_GA)))
                ph_merge.load(sp, i, 4, w_cols(w_br_ssm, 0, KU, i * P))
                ph_merge.load(sp, i, 5, w_cols(w_br_att, 0, KU, i * P))
            for j in range(4):
                ph_out.load(sp, 0, j, w_cols(w_out, KU * (j % 2), KU, (j // 2) * P))
            sp.wait_ge(s_all, reached("merged"))
            for t in range(4):
                if t >= 2:
                    sp.wait_ge(s_x2t, 4 * (t - 1))
                sp.dma_start(x_again[:, t % 2, :], x_prompt[0, t * P:(t + 1) * P, :]).then_inc(s_x2[t % 2], 16)
                if t == 0:
                    sp.dma_start(x_smp2[:, :], x_sample.rearrange("b s d -> (b s) d")).then_inc(s_xs2, 16)
            with sp.Fori(1, ph_out.times) as i:
                for j in range(4):
                    ph_out.load(sp, i, j, w_cols(w_out, KU * (j % 2), KU, i * (2 * P) + (j // 2) * P))
            with sp.Fori(0, FF_BLOCKS) as n:
                up, down = (p.in_block(n) for p in ph_ffn)
                with sp.Fori(0, up.times) as i:
                    for j in range(4):
                        up.load(sp, i, j, w_cols(w_up if j // 2 else w_gate, KU * (j % 2), KU,
                                                 n * (FF_TILES * P) + i * P))
                with sp.Fori(0, down.times) as i:
                    for j in range(4):
                        k0, nk = FF_UNITS[j % 2]
                        down.load(sp, i, j, w_rows(w_down, n * (FF_TILES * P) + k0 * P, nk, i * (2 * P) + (j // 2) * P))
            ph_end.load(sp, 0, 0, w_cols(w_glu, 0, 1, 0))
            for t in range(5):
                sp.wait_ge(s_yca, min(2 * t + 2, 8))
                sp.wait_ge(s_ycd, 2 * t + 2 if t < 4 else 9)
                if t < 4:
                    sp.dma_start(y_prompt[0, t * P:(t + 1) * P, :], y_nat[:, t % 2, :]).then_inc(s_yst[t % 2], 16)
                else:
                    sp.dma_start(y_sample.rearrange("b s d -> (b s) d"), y_nat[0:NS, 0, :]).then_inc(s_yst[0], 16)
            sp.wait_ge(s_yst[0], 48)
            sp.wait_ge(s_yst[1], 32)

        @block.gpsimd
        def _(pool):
            for s in (
                    s_bias, s_bm, s_bu, s_buc, s_cb, s_ch, s_cm, *s_dn, s_dp, s_ev, s_ex, s_ga, s_gg,
                    s_gs, s_h, s_hh, s_hs, s_hid, s_hl, s_kst, s_kv, s_kvc, s_m, s_mg, s_mx, s_nm, s_oc,
                    s_pr, s_pt, s_ptc, s_pv, s_pvp, s_pw, s_qk, s_qn, s_qrs, s_qsum, *s_res, s_rs2,
                    s_sc, s_sco, s_silu, s_sm, s_stage, s_sx, s_ta, s_tca, s_tcd, s_td, s_tt,
                    s_ub, s_uc, *s_uev, s_up, s_yev, s_ys):
                pool.sem_inc(s, 1)
            pool.memset(ident[:, :], 0.0).then_inc(s_ident, 1)
            pool.memset(ones[:, :], 1.0)
            pool.memset(consts[:, 0:1], 0.0)
            pool.memset(consts[:, 1:2], EPS)
            pool.iota(par_i[:, 0:1], [[0, 1]], base=0, channel_multiplier=1).then_inc(s_ident, 1)
            pool.wait_ge(s_ident, 2)
            pool.affine_select(out=ident[:, :], in_=ident[:, :], compare_op=ALU.not_equal, fill=1.0,
                               base=0, pattern=[[-1, P]], channel_multiplier=1).then_inc(s_ident, 1)
            pool.sem_inc(s_lo, RAW)
            barrier(pool, "setup")
            pool.wait_ge(s_hi, RAW + 1)
            pool.tensor_tensor(w_lo[:, 0, :, :], raw[:, 0, :, :], w_hi[:, 0, :, :].bitcast(F32),
                               ALU.subtract).then_inc(s_lo, 1)
            norm_pool(pool, "mix")
            barrier(pool, "normed")
            for j in range(1, 3):
                ph_f.split_lo(pool, 0, j)
            with pool.Fori(0, ph_u.times) as i:
                for j in range(1, 5):
                    ph_u.split_lo(pool, i, j)
            barrier(pool, "u")

            def head_norm(i, n, t):
                pool.wait_ge(s_pw, i * 2 + n + 2)
                pool.tensor_tensor(tile_of(t, i), tile_of(t, i), tile_of(v, i), ALU.mult).then_inc(s_qn, 1)

            def sample_steps(i, j):
                hr, hi = h_re[:, j % 2, :], h_im[:, j % 2, :]
                at_tile = st_s[:, :, :, bass.ds(i * 4 + j, 1)].rearrange("p c b s -> p c (b s)")
                pool.wait_ge(s_buc, i * 8 + 2 * j + 3)
                pool.wait_ge(s_up, i + 2)
                settle(pool, "pool")
                pool.tensor_copy(st_w[:, :, :], at_tile).then_inc(s_steps, 1)
                pool.wait_ge(s_steps, 1)
                n = 1
                f = [use_p[:, 0, c, j:j + 1] for c in range(3)]
                for step in range(DEC_SEQ):
                    dst = h_both[:, :, j % 2, SEQ + step:T:DEC_SEQ]
                    src = h_both[:, :, j % 2, SEQ + step - 1:T:DEC_SEQ] if step else st_w[:, :, :]
                    pool.tensor_scalar(prods[:, 0, :, :], src, f[0], None, ALU.mult).then_inc(s_steps, 1)
                    pool.tensor_scalar(prods[:, 1, 0, :], src[:, 1, :], f[2], None, ALU.mult).then_inc(s_steps, 1)
                    pool.tensor_scalar(prods[:, 1, 1, :], src[:, 0, :], f[1], None, ALU.mult).then_inc(s_steps, 1)
                    for c in range(2):
                        pool.wait_ge(s_steps, n + 3 + c)
                        pool.tensor_tensor(dst, dst, prods[:, c, :, :], ALU.add).then_inc(s_steps, 1)
                    n += 5
                    if step < DEC_SEQ - 1:
                        pool.wait_ge(s_steps, n)
                pool.wait_ge(s_steps, n)
                for c, x in enumerate((hr, hi)):
                    pool.tensor_copy(st_s[:, c, :, bass.ds(i * 4 + j, 1)].rearrange("p b s -> p (b s)"),
                                     x[:, SEQ + DEC_SEQ - 1:T:DEC_SEQ]).then_inc(s_steps, 1)
                pool.wait_ge(s_steps, n + 2)
                pool.sem_clear(s_steps)
                pool.sem_inc(s_hs, 1)

            with pool.Fori(0, HEADS) as i:
                pool.wait_ge(s_bu, i * 8 + 1)
                pool.tensor_copy(use_b[:, :, :], tab_b[:, bass.ds(i, 1), :, :].rearrange("p a c n -> p (a c) n"))\
                    .then_inc(s_ub, 1)
                pool.tensor_copy(use_u[:, :], tile_of(u, i)).then_inc(s_ub, 1)
                pool.wait_ge(s_h, i * 4 + 1)
                pool.tensor_copy(use_p[:, :, :, :].rearrange("p l c s -> p (l c) s"),
                                 pow_a[:, :, :, bass.ds(i * 4, 4)].rearrange("p l c s -> p (l c) s"))\
                    .then_inc(s_up, 1)
                ph_qkv.split_lo(pool, i, 1)
                sample_steps(i, 0)
                ph_qkv.split_lo(pool, i, 2)
                sample_steps(i, 1)
                pool.wait_ge(s_ch, i * 4 + 1)
                pool.tensor_copy(use_c[:, :, :], tab_c[:, bass.ds(i, 1), :, :].rearrange("p a c n -> p (a c) n"))\
                    .then_inc(s_uc, 1)
                ph_qkv.split_lo(pool, i, 3)
                ph_qkv.split_lo(pool, i, 4)
                head_norm(i, 0, q)
                sample_steps(i, 2)
                ph_qkv.split_lo(pool, i, 5)
                ph_qkv.split_lo(pool, i, 6)
                sample_steps(i, 3)
                head_norm(i, 1, k)
            barrier(pool, "qkv")
            barrier(pool, "states")
            pool.memset(causal[:, :], 0.0).then_inc(s_causal, 1)
            pool.wait_ge(s_causal, 1)
            pool.affine_select(out=causal[:, :], in_=causal[:, :], compare_op=ALU.is_ge, fill=NEG, base=0,
                               pattern=[[-1, P]], channel_multiplier=1).then_inc(s_causal, 1)
            with pool.Fori(0, HEADS // 2) as i:
                for e in range(2):
                    pool.wait_ge(s_kv, i * 2 + 1)
                    pool.wait_ge(s_qk, i * 2 + 1)
                    for c, t in enumerate((q, k, v)):
                        pool.tensor_copy(stage[:, e, c, :], tile_of(t, i * 2 + e)).then_inc(s_stage, 1)
            pool.wait_ge(s_kst, 64 * HEADS + 1)
            pool.wait_ge(s_store, 16 * 6)
            barrier(pool, "prompt")
            pool.memset(later[:, :], 1.0).then_inc(s_pool_c, 1)
            pool.memset(mask32[:, :], 0.0)
            pool.memset(page_of[:, :], 1.0)
            pool.memset(zeros[:, :], 0.0)
            pool.memset(new_pr[:, :, :], 0.0).then_inc(s_pool_c, 1)
            pool.wait_ge(s_pool_c, 2)
            pool.affine_select(out=later[:, :], in_=later[:, :], compare_op=ALU.is_gt, fill=0.0, base=0,
                               pattern=[[-1, PAGE]], channel_multiplier=1)
            pool.affine_select(out=mask32[:, 0:NS], in_=mask32[:, 0:NS], compare_op=ALU.is_ge, fill=NEG, base=0,
                               pattern=[[-1, NS]], channel_multiplier=1)
            pool.affine_select(out=mask32[:, NS:NS + DEC_BATCH], in_=mask32[:, NS:NS + DEC_BATCH],
                               compare_op=ALU.is_ge, fill=NEG, base=0, pattern=[[-DEC_SEQ, DEC_BATCH]],
                               channel_multiplier=1)
            pool.affine_select(out=page_of[:, :], in_=page_of[:, :], compare_op=ALU.is_ge, fill=0.0, base=0,
                               pattern=[[-HEADS, N_PAGES]], channel_multiplier=1).then_inc(s_pool_c, 1)
            pool.wait_ge(s_pool_c, 3)
            pool.affine_select(out=page_of[:, :], in_=page_of[:, :], compare_op=ALU.is_ge, fill=0.0, base=HEADS - 1,
                               pattern=[[HEADS, N_PAGES]], channel_multiplier=-1)
            pool.affine_select(out=mask32[:, 0:NS].rearrange("p (b s) -> p b s", s=DEC_SEQ),
                               in_=mask32[:, 0:NS].rearrange("p (b s) -> p b s", s=DEC_SEQ), compare_op=ALU.is_ge,
                               fill=NEG, base=DEC_SEQ - 1, pattern=[[DEC_SEQ, DEC_BATCH], [0, DEC_SEQ]],
                               channel_multiplier=-1)
            pool.affine_select(out=mask32[:, NS:NS + DEC_BATCH], in_=mask32[:, NS:NS + DEC_BATCH],
                               compare_op=ALU.is_ge, fill=NEG, base=DEC_SEQ - 1, pattern=[[DEC_SEQ, DEC_BATCH]],
                               channel_multiplier=-1).then_inc(s_pool_c, 1)
            pool.wait_ge(s_pool_c, 4)
            pool.wait_ge(s_spc, 1)
            with pool.Fori(0, DEC_BATCH) as b:
                for pr in range(N_PAGES // 2):
                    pool.wait_ge(s_sco, b * N_PAGES + (2 * max(pr - 3, 0) + 1))
                    settle(pool, "pool")
                    for e in range(2):
                        ins = pool.tensor_tensor(decay_p[:, pr % 4, e, :],
                                                 decay[:, bass.ds(b, 1), :].rearrange("p a n -> p (a n)"),
                                                 page_of[:, 2 * pr + e:2 * pr + e + 1].to_broadcast([P, PAGE]),
                                                 ALU.mult)
                    ins.then_inc(s_dp, 1)
            barrier(pool, "sample")
            for t in range(0, KH, 2):
                pool.wait_ge(s_y1h, t + 1)
                pool.tensor_tensor(y1_lo[:, t, :], u[:, t, :], y1_hi[:, t, :].bitcast(F32), ALU.subtract)\
                    .then_inc(s_y1l, 1)
            with pool.Fori(0, ph_glu.times) as i:
                for j in range(1, 5):
                    ph_glu.split_lo(pool, i, j)
            with pool.Fori(0, ph_merge.times) as i:
                for j in range(1, 7):
                    ph_merge.split_lo(pool, i, j)
            barrier(pool, "merged")
            for t in range(0, KD, 2):
                pool.wait_ge(s_mhi, t // 2 + 1)
                pool.tensor_tensor(xn_lo[:, t, :], merged[:, t, :], xn_hi[:, t, :].bitcast(F32), ALU.subtract)\
                    .then_inc(s_mlo, 1)
            with pool.Fori(0, ph_out.times) as i:
                for j in range(1, 5):
                    ph_out.split_lo(pool, i, j)
            barrier(pool, "out")
            norm_pool(pool, "ffn")
            barrier(pool, "ffn_normed")
            with pool.Fori(0, FF_BLOCKS) as n:
                up, down = (p.in_block(n) for p in ph_ffn)
                with pool.Fori(0, up.times) as i:
                    for j in range(1, 5):
                        up.split_lo(pool, i, j)
                    pool.wait_ge(s_hh, n * FF_TILES + i + 2)
                    pool.tensor_tensor(tile_of(hid_lo, i), hid[:, :], tile_of(hid_hi, i).bitcast(F32), ALU.subtract)\
                        .then_inc(s_hl, 1)
                with pool.Fori(0, down.times) as i:
                    for j in range(1, 5):
                        down.split_lo(pool, i, j, FF_SPLIT[j])
            barrier(pool, "ffn")

        @block.scalar
        def _(act):
            act.sem_inc(s_hi, RAW)
            barrier(act, "setup")
            act.wait_ge(s_landed[0], 16)
            act.activation(w_hi[:, 0, :, :], raw[:, 0, :, :], ACT.Copy).then_inc(s_hi, 1)
            norm_act(act, "mix")
            barrier(act, "normed")
            for j in range(1, 3):
                ph_f.split_hi(act, 0, j)

            def u_tiles(lo, hi):
                with act.Fori(lo, hi) as i:
                    ph_u.split_hi(act, i, 1)
                    ph_u.split_hi(act, i, 2)
                    for c in range(2):
                        ph_u.split_hi(act, i, 3 + c)
                        act.wait_ge(s_used, ph_u.used(i, 2 * c + 1))
                        settle(act, "act")
                        act.activation(two(u[:, bass.ds(i * 2 + c, 1), :].rearrange("p a n -> p (a n)")), pair(c), ACT.Copy)\
                           .then_inc(s_uev[c], 1)

            u_tiles(0, 2)
            act.wait_ge(s_dve_s, 1)
            act.activation(nt(N_SIN), nt(N_R), ACT.Sin).then_inc(s_exp, 1)
            act.activation(nt(N_COS), nt(N_ABS), ACT.Sin).then_inc(s_exp, 1)
            u_tiles(2, 4)
            barrier(act, "u")

            def bu_copy(i, n):
                j = n // 2
                act.wait_ge(s_bu, i * 8 + n + 2)
                act.wait_ge(s_ch, i * 4 + (max(j - 1, 0) + 1))
                act.activation(two((h_im if n % 2 else h_re)[:, j % 2, :]), pair(C), ACT.Copy)\
                   .then_inc(s_buc, 1)

            def root(i, n):
                act.wait_ge(s_qsum, i * 2 + n + 2)
                settle(act, "act")
                act.activation(two(tile_of(v, i)), pair(C), ACT.Sqrt, scale=1.0 / P, bias=consts[:, 1:2])\
                   .then_inc(s_qrs, 1)

            act.preload_act_table(ACT.Sqrt)
            with act.Fori(0, HEADS) as i:
                bu_copy(i, 0)
                bu_copy(i, 1)
                ph_qkv.split_hi(act, i, 1)
                bu_copy(i, 2)
                bu_copy(i, 3)
                ph_qkv.split_hi(act, i, 2)
                act.wait_ge(s_m, i * 3 + 2)
                act.activation(two(tile_of(q, i)), pair(A), ACT.Copy, scale=vecs[:, V_QG:V_QG + 1])
                act.activation(two(tile_of(v, i)), pair(A), ACT.Square).then_inc(s_ev, 1)
                ph_qkv.split_hi(act, i, 3)
                ph_qkv.split_hi(act, i, 4)
                bu_copy(i, 4)
                root(i, 0)
                ph_qkv.split_hi(act, i, 5)
                bu_copy(i, 5)
                act.wait_ge(s_m, i * 3 + 3)
                act.activation(two(tile_of(k, i)), pair(B), ACT.Copy, scale=vecs[:, V_KG:V_KG + 1])
                act.wait_ge(s_qn, i * 2 + 2)
                settle(act, "act")
                act.activation(two(tile_of(v, i)), pair(B), ACT.Square).then_inc(s_ev, 1)
                bu_copy(i, 6)
                ph_qkv.split_hi(act, i, 6)
                root(i, 1)
                bu_copy(i, 7)
                act.wait_ge(s_m, i * 3 + 4)
                act.wait_ge(s_qn, i * 2 + 3)
                settle(act, "act")
                act.activation(two(tile_of(v, i)), pair(A), ACT.Copy).then_inc(s_ev, 1)
            barrier(act, "qkv")
            barrier(act, "states")
            act.preload_act_table(ACT.Exp)
            with act.Fori(0, HEADS) as h:
                act.wait_ge(s_cb, h + 1)
                act.activation(cm[:, :], cum[:, :], ACT.Copy, scale=ident[0:HEADS, bass.ds(h, 1)])\
                   .then_inc(s_cm, 1)
                act.wait_ge(s_cb, h + 2)
                act.wait_ge(s_pt, h * 3 + 1)
                for b in ORDER:
                    act.activation(prob[:, off[b]:off[b + 1]], ps[:, 7, 0:(b + 1) * P], ACT.Identity, scale=-1.0,
                                   bias=lf_nat[:, b, 1, bass.ds(h, 1)]).then_inc(s_bias, 1)
                act.wait_ge(s_kv, h + 2)
                act.wait_ge(s_kst, h * 64 + 1)
                act.activation(nat_kv[:, 0, :, :].rearrange("p a n -> p (a n)"), ps[:, 4, :], ACT.Copy)
                act.activation(nat_kv[:, 1, :, :].rearrange("p a n -> p (a n)"), ps[:, 5, :], ACT.Copy)
                act.activation(vs_nat[:, bass.ds(h, 1), :].rearrange("p a n -> p (a n)"), ps[0:NS, 6, P:2 * P], ACT.Copy)
                act.activation(nat_s[:, :, :].rearrange("p a n -> p (a n)"), ps[0:NS, 6, 0:2 * P], ACT.Copy)\
                   .then_inc(s_kvc, 1)
                for n, b in enumerate(ORDER):
                    act.wait_ge(s_nm, h * QB + (n + 2))
                    act.activation(prob[:, off[b]:off[b + 1]], prob[:, off[b]:off[b + 1]], ACT.Exp,
                                   bias=stat[:, 0, b:b + 1], accum_out=stat[:, 1, b:b + 1]).then_inc(s_ex, 1)
                act.wait_ge(s_pv, h + 2)
                act.activation(q[:, bass.ds(h, 1), 0:SEQ].rearrange("p a n -> p (a n)"), ps[:, 6, :], ACT.Copy)\
                   .then_inc(s_oc, 1)
            barrier(act, "prompt")
            act.preload_act_table(ACT.Exp)
            with act.Fori(0, DEC_BATCH) as b:
                def turned(r, dst):
                    act.wait_ge(s_tt, b * ROUNDS + (r + 1 + 1))
                    act.activation(dst, ps[:, 2 * (r % 2), :], ACT.Copy).then_inc(s_tca, 1)

                def copy_scores(pr):
                    act.wait_ge(s_sco, b * N_PAGES + 2 * (pr + 1) + 1)
                    for g in range(2):
                        ins = act.activation(scores[:, g, pr * 256:(pr + 1) * 256], ps[:, 4, 256 * g:256 * g + 256],
                                             ACT.Identity, bias=c_query[:, g:g + 1])
                    ins.then_inc(s_ta, 1)

                for p in range(N_PAGES):
                    act.wait_ge(s_sco, b * N_PAGES + (max(p - 1, 0) + 1))
                    turned(p, key_t[:, p % 2, 0, :])
                    if p % 4 == 3:
                        copy_scores(p // 2 - 1)
                def exp_group(gr):
                    for g in range(2):
                        t = scores[:, g, gr * 512:(gr + 1) * 512]
                        ins = act.activation(t, t, ACT.Exp, bias=s_nmax[:, g:g + 1], accum_out=exp_part[:, g, gr:gr + 1])
                    ins.then_inc(s_sx, 1)

                def prob_turned(gr):
                    act.wait_ge(s_pvp, b * N_PAGES + (N_PAGES + 4 * max(gr - 1, 0) + 1))
                    turned(N_PAGES + gr, prob_st[:, gr % 2, 0, :])

                act.wait_ge(s_sm, b * 9 + 7)
                exp_group(0)
                for gr in range(1, GROUPS):
                    exp_group(gr)
                    prob_turned(gr - 1)
                for g in range(2):
                    ins = act.activation(new_ex[:, g, :], new_sc[:, g, :], ACT.Exp, bias=s_nmax[:, g:g + 1],
                                         accum_out=exp_part[:, g, GROUPS:GROUPS + 1])
                ins.then_inc(s_sx, 1)
                prob_turned(GROUPS - 1)
            barrier(act, "sample")
            for t in range(KH):
                act.activation(u[:, t, :], u[:, t, :], ACT.Gelu).then_inc(s_gelu, 1)
            for t in range(KH):
                act.wait_ge(s_gelu, t + 1)
                act.activation(y1_hi[:, t, :], u[:, t, :], ACT.Copy).then_inc(s_y1h, 1)
            act.preload_act_table(ACT.Sigmoid)
            with act.Fori(0, ph_glu.times) as i:
                for j in range(4):
                    ph_glu.split_hi(act, i, j + 1)
                    act.wait_ge(s_used, ph_glu.used(i, j))
                    act.wait_ge(s_ys, (i * 4 + j - 1 if j >= 2 else i * 4) + 1)
                    act.activation(two(glu_gate[:, j % 2, :]), pair(j), ACT.Sigmoid,
                                   bias=vecs[:, bass.ds(i * 4 + (V_BGLU + j), 1)]).then_inc(s_gg, 1)
            act.wait_ge(s_ys, KH + 1)
            with act.Fori(0, ph_merge.times) as i:
                ph_merge.split_hi(act, i, 1)
                ph_merge.split_hi(act, i, 2)
                ph_merge.split_hi(act, i, 3)
                act.wait_ge(s_used, ph_merge.used(i, 1))
                act.activation(two(tile_of(merged, i)), pair(A), ACT.Sigmoid).then_inc(s_gs, 1)
                ph_merge.split_hi(act, i, 4)
                ph_merge.split_hi(act, i, 5)
                act.wait_ge(s_used, ph_merge.used(i, 3))
                act.wait_ge(s_mg, i * 3 + 1)
                act.activation(two(att_gate[:, :]), pair(B), ACT.Sigmoid).then_inc(s_ga, 1)
                ph_merge.split_hi(act, i, 6)
            barrier(act, "merged")
            for t in range(0, KD, 2):
                act.activation(xn_hi[:, t, :], merged[:, t, :], ACT.Copy).then_inc(s_mhi, 1)
            for t in range(4):
                for g in range(4):
                    act.wait_ge(s_x2t, 4 * t + g + 1)
                    act.activation(x_t[:, 4 * g:4 * g + 4, t * P:(t + 1) * P],
                                   ps[:, g if t % 2 else 4 + g, :].rearrange("p (c n) -> p c n", n=P), ACT.Copy)\
                       .then_inc(s_x2c, 1)
            act.wait_ge(s_x2t, 17)
            act.activation(x_t[:, :, SEQ:T], ps[:, 4, :].rearrange("p (c n) -> p c n", n=NS), ACT.Copy).then_inc(s_x2c, 1)
            with act.Fori(0, ph_out.times) as i:
                for j in range(1, 5):
                    ph_out.split_hi(act, i, j)
            barrier(act, "out")
            norm_act(act, "ffn")
            barrier(act, "ffn_normed")
            act.preload_act_table(ACT.Silu)
            with act.Fori(0, FF_BLOCKS) as n:
                up, down = (p.in_block(n) for p in ph_ffn)
                with act.Fori(0, up.times) as i:
                    up.split_hi(act, i, 1)
                    up.split_hi(act, i, 2)
                    up.split_hi(act, i, 3)
                    act.wait_ge(s_used, up.used(i, 1))
                    act.activation(two(ff_act[:, :]), pair(A), ACT.Silu).then_inc(s_silu, 1)
                    up.split_hi(act, i, 4)
                    act.wait_ge(s_hid, n * FF_TILES + i + 2)
                    act.activation(tile_of(hid_hi, i), hid[:, :], ACT.Copy).then_inc(s_hh, 1)
                with act.Fori(0, down.times) as i:
                    for j in range(1, 5):
                        down.split_hi(act, i, j, FF_SPLIT[j])
            barrier(act, "ffn")
            for t in range(4):
                for g in range(2):
                    act.wait_ge(s_yt, 4 * t + 2 * g + 1)
                    if t >= 2:
                        act.wait_ge(s_yst[t % 2], 16)
                    act.activation(y_nat[:, t % 2, 2 * g * 512:(2 * g + 1) * 512], ps[:, 4 * (t % 2) + 2 * g, :], ACT.Copy)\
                       .then_inc(s_yca, 1)

        @block.vector
        def _(eng):
            mul = lambda o, a, b: dve(eng, eng.tensor_tensor(o, a, b, ALU.mult))
            add = lambda o, a, b: dve(eng, eng.tensor_tensor(o, a, b, ALU.add))
            sub = lambda o, a, b: dve(eng, eng.tensor_tensor(o, a, b, ALU.subtract))

            def exp_exact(out, x, whole, bits):
                step = lambda ins: dve(eng, ins)
                step(eng.tensor_scalar(whole, x, 1 / math.log(2), MAGIC, ALU.mult, ALU.add))
                step(eng.tensor_scalar(whole, whole, -MAGIC, None, ALU.add))
                step(eng.scalar_tensor_tensor(x, whole, -0.693359375, x, ALU.mult, ALU.add))
                step(eng.scalar_tensor_tensor(x, whole, 0.693359375 - math.log(2), x, ALU.mult, ALU.add))
                step(eng.tensor_scalar(out, x, 1 / 5040, None, ALU.mult))
                for f in (720, 120, 24, 6, 2, 1):
                    step(eng.scalar_tensor_tensor(out, out, 1 / f, x, ALU.add, ALU.mult))
                step(eng.tensor_scalar(out, out, 1.0, None, ALU.add))
                step(eng.tensor_scalar(whole, whole, 127.0, None, ALU.add))
                step(eng.tensor_copy(bits, whole))
                step(eng.tensor_scalar(bits, bits, 23, None, ALU.logical_shift_left))
                step(eng.tensor_tensor(out, out, bits.bitcast(F32), ALU.mult))

            eng.wait_ge(s_setup_t, 1)
            dve(eng, eng.tensor_copy(vecs[:, :], ps[:, 0, 0:50]))
            eng.sem_inc(s_setup_c, 1)
            for t in range(4):
                for g in range(4):
                    eng.wait_ge(s_xt, 4 * t + g + 1)
                    eng.tensor_copy(x_t[:, 4 * g:4 * g + 4, t * P:(t + 1) * P],
                                    ps[:, g if t % 2 else 4 + g, :].rearrange("p (c n) -> p c n", n=P)).then_inc(s_xc, 1)
            eng.wait_ge(s_xt, 17)
            eng.tensor_copy(x_t[:, :, SEQ:T], ps[:, 4, :].rearrange("p (c n) -> p c n", n=NS)).then_inc(s_xc, 1)
            barrier(eng, "setup")
            norm_dve(eng, "mix")
            barrier(eng, "normed")
            z, e, w2, s2 = (lf_w[:, n, :] for n in range(4))
            eng.wait_ge(s_fm, 1)
            eng.wait_ge(s_small, 16 * 6)
            dve(eng, eng.tensor_scalar(two(z), pair(C)[0:HEADS], bf_col[:, :], None, ALU.add))
            dve(eng, eng.scalar_tensor_tensor(e, z, -1.0, z, ALU.mult, ALU.min))
            dve(eng, eng.tensor_scalar(z, z, 0.0, None, ALU.min))
            dve(eng, eng.tensor_scalar(e, e, -87.0, None, ALU.max))
            exp_exact(w2, e, s2, lf_i[:, :])
            dve(eng, eng.tensor_copy(e, w2))
            dve(eng, eng.tensor_scalar(w2, e, 2.0, None, ALU.add))
            dve(eng, eng.reciprocal(w2, w2))
            mul(e, e, w2)
            mul(s2, e, e)
            dve(eng, eng.tensor_scalar(w2, s2, 1.0 / 15, None, ALU.mult))
            for n in range(13, 1, -2):
                dve(eng, eng.scalar_tensor_tensor(w2, w2, 1.0 / n, s2, ALU.add, ALU.mult))
            dve(eng, eng.scalar_tensor_tensor(w2, w2, 1.0, e, ALU.add, ALU.mult))
            dve(eng, eng.scalar_tensor_tensor(z, w2, -2.0, z, ALU.mult, ALU.add))
            dve(eng, eng.memset(e, 1.0))
            dve(eng, eng.memset(e[:, SEQ:T:DEC_SEQ], 0.0))
            dve(eng, eng.tensor_tensor_scan(cum[:, :], e, z, 0.0, ALU.mult, ALU.add))
            eng.sem_inc(s_lf, 1)
            eng.wait_ge(s_dt, 16 * 3)
            eng.wait_ge(s_small, 16 * 6)
            exp_exact(dt_w[:, 0, :], dt2[:, :], dt_w[:, 1, :], dt_i[:, :])
            dve(eng, eng.tensor_copy(nt(N_DT).rearrange("s (g p) -> s g p", g=2),
                                     dt_w[:, 0, :].rearrange("s (g o) -> s g o", o=1).to_broadcast([STILES, 2, 64])))
            mul(nt(N_T1), nt(N_DT), nt(N_ARE))
            exp_exact(nt(N_MAG), nt(N_T1), nt(N_T2), nat_i[:, :])
            mul(nt(N_ANG), nt(N_DT), nt(N_AIM))
            dve(eng, eng.tensor_scalar(nt(N_K), nt(N_ANG), 1.0 / TWO_PI, MAGIC, ALU.mult, ALU.add))
            dve(eng, eng.tensor_scalar(nt(N_K), nt(N_K), -MAGIC, None, ALU.add))
            dve(eng, eng.tensor_copy(nt(N_R), nt(N_ANG)))
            for part in two_pi_parts():
                dve(eng, eng.scalar_tensor_tensor(nt(N_R), nt(N_K), -part, nt(N_R), ALU.mult, ALU.add))
            dve(eng, eng.tensor_scalar(nt(N_R), nt(N_R), 3.1415925, -3.1415925, ALU.min, ALU.max))
            dve(eng, eng.scalar_tensor_tensor(nt(N_ABS), nt(N_R), -1.0, nt(N_R), ALU.mult, ALU.max))
            dve(eng, eng.tensor_scalar(nt(N_ABS), nt(N_ABS), -1.0, math.pi / 2, ALU.mult, ALU.add))
            eng.sem_inc(s_dve_s, 1)
            eng.wait_ge(s_exp, 2)
            mul(nt(N_ABR), nt(N_MAG), nt(N_COS))
            mul(nt(N_ABI), nt(N_MAG), nt(N_SIN))
            dve(eng, eng.tensor_scalar(nt(N_ER), nt(N_ABR), -1.0, None, ALU.add))
            mul(nt(N_T1), nt(N_ARE), nt(N_ARE))
            mul(nt(N_T2), nt(N_AIM), nt(N_AIM))
            add(nt(N_DEN), nt(N_T1), nt(N_T2))
            dve(eng, eng.reciprocal(nt(N_INV), nt(N_DEN)))
            mul(nt(N_T1), nt(N_ER), nt(N_ARE))
            mul(nt(N_T2), nt(N_ABI), nt(N_AIM))
            add(nt(N_T1), nt(N_T1), nt(N_T2))
            mul(nt(N_FR), nt(N_T1), nt(N_INV))
            mul(nt(N_T1), nt(N_ABI), nt(N_ARE))
            mul(nt(N_T2), nt(N_ER), nt(N_AIM))
            sub(nt(N_T1), nt(N_T1), nt(N_T2))
            mul(nt(N_FI), nt(N_T1), nt(N_INV))
            eng.sem_inc(s_dve_s, 1)
            eng.wait_ge(s_setup_t, 2)
            for c in range(2):
                dve(eng, eng.tensor_copy(pow_a[:, 0, c, :], ps[:, 6, 64 + 32 * c:96 + 32 * c]))
                dve(eng, eng.tensor_copy(f_col[:, c, :], ps[:, 6, 128 + 32 * c:160 + 32 * c]))
                dve(eng, eng.tensor_copy(st_s[:, c, :, :].rearrange("p b s -> p (b s)"),
                                         ps[:, 7, 256 * c:256 * c + 256]))
            sq_a, sq_b = b_tmp[:, 0, :, 0], b_tmp[:, 0, :, 1]
            for lv in range(LEVELS):
                dve(eng, eng.tensor_scalar(pow_a[:, lv, 2, :], pow_a[:, lv, 1, :], -1.0, None, ALU.mult))
                if lv + 1 < LEVELS:
                    mul(sq_a, pow_a[:, lv, 0, :], pow_a[:, lv, 0, :])
                    mul(sq_b, pow_a[:, lv, 1, :], pow_a[:, lv, 1, :])
                    sub(pow_a[:, lv + 1, 0, :], sq_a, sq_b)
                    mul(sq_a, pow_a[:, lv, 0, :], pow_a[:, lv, 1, :])
                    add(pow_a[:, lv + 1, 1, :], sq_a, sq_a)
            dve(eng, eng.memset(b_pad[:, :, :, :, :, :], 0.0))
            fb = [f_col[:, c, :].rearrange("p (s o) -> p s o", o=1).to_broadcast([P, STILES, 16]) for c in range(2)]
            for c, (x0, x1, op) in enumerate(((0, 1, ALU.subtract), (1, 0, ALU.add))):
                mul(b_tmp[:, 0, :, :], b_nat[:, x0, :, :], fb[0])
                mul(b_tmp[:, 1, :, :], b_nat[:, x1, :, :], fb[1])
                for g in range(2):
                    r = slice(64 * g, 64 * g + 64)
                    dve(eng, eng.tensor_tensor(
                        b_pad[r, c, :, :, g, :].rearrange("p t j c -> p (t j) c"),
                        b_tmp[r, 0, :, :], b_tmp[r, 1, :, :], op))
            eng.wait_ge(s_ident, 2)
            eng.wait_ge(s_cn, 32)
            dve(eng, eng.tensor_scalar(par_i[:, 1:2], par_i[:, 0:1], 4, 1, ALU.logical_shift_right, ALU.bitwise_and))
            dve(eng, eng.tensor_copy(consts[:, 3:4], par_i[:, 1:2]))
            dve(eng, eng.tensor_scalar(consts[:, 2:3], consts[:, 3:4], -1.0, 1.0, ALU.mult, ALU.add))
            for c, sign in ((0, 1.0), (1, -1.0)):
                for g in range(2):
                    dve(eng, eng.tensor_scalar(c_pad[:, c, :, g, :], c_nat[:, c, :, :],
                                               consts[:, 2 + g:3 + g], sign, ALU.mult, ALU.mult))
            eng.sem_inc(s_dve_s, 1)
            n = 0
            for dst in (tab_b, tab_c):
                for c in range(2):
                    for half in range(2):
                        n += 1
                        eng.wait_ge(s_setup_t, 2 + n)
                        dve(eng, eng.tensor_copy(dst[:, 4 * half:4 * half + 4, c, :],
                                                 ps[:, 4 + n % 4, :].rearrange("p (t n) -> p t n", n=P)))
                        eng.sem_inc(s_setup_c, 1)
            eng.wait_ge(s_lft, 1)
            dve(eng, eng.tensor_copy(lf_nat[:, 0:4, :, :].rearrange("p a c h -> p (a c h)"), ps[:, 7, 0:64]))
            dve(eng, eng.tensor_copy(lf_nat[0:NS, 4, :, :].rearrange("p c h -> p (c h)"), ps[0:NS, 7, 64:80]))
            barrier(eng, "u")

            def scan_op(n, out, src, factor):
                if n >= 2:
                    eng.wait_ge(s_scan, n - 1)
                eng.scalar_tensor_tensor(out, src, factor, out, ALU.mult, ALU.add).then_inc(s_scan, 1)

            def scan(i, j):
                b = j % 2
                hr, hi = h_re[:, b, :], h_im[:, b, :]
                s = i * 4 + j
                eng.wait_ge(s_buc, i * 8 + 2 * j + 3)
                steps = []
                for lv in range(LEVELS):
                    d = 1 << lv
                    steps.append((lv, slice(2 * d - 1, SEQ, 2 * d), slice(d - 1, SEQ, 2 * d)))
                for lv in range(LEVELS - 2, -1, -1):
                    d = 1 << lv
                    steps.append((lv, slice(3 * d - 1, SEQ, 2 * d), slice(2 * d - 1, SEQ - 1, 2 * d)))
                n = 0
                for lv, dst, src in steps:
                    f = [use_p[:, lv, c, j:j + 1] for c in range(3)]
                    sr, si = hr[:, src], hi[:, src]
                    for out, sx, fx in ((hr[:, dst], sr, f[0]), (hi[:, dst], si, f[0]),
                                        (hr[:, dst], si, f[2]), (hi[:, dst], sr, f[1])):
                        scan_op(n, out, sx, fx)
                        n += 1
                eng.wait_ge(s_scan, n)
                for c, x in ((0, hr), (1, hi)):
                    eng.tensor_copy(st_p[:, c, bass.ds(s, 1)], x[:, SEQ - 1:SEQ]).then_inc(s_scan, 1)
                eng.wait_ge(s_scan, n + 2)
                eng.sem_clear(s_scan)
                eng.sem_inc(s_h, 1)


            def head_rstd(i, n):
                eng.wait_ge(s_qrs, i * 2 + n + 2)
                settle(eng, "dve")
                eng.reciprocal(tile_of(v, i), tile_of(v, i)).then_inc(s_pw, 1)

            with eng.Fori(0, HEADS) as i:
                eng.wait_ge(s_up, i + 2)
                scan(i, 0)
                scan(i, 1)
                head_rstd(i, 0)
                scan(i, 2)
                head_rstd(i, 1)
                scan(i, 3)
                eng.wait_ge(s_ch, i * 4 + 5)
                eng.scalar_tensor_tensor(two(tile_of(u, i)), two(tile_of(u, i)), vecs[:, bass.ds(i + V_D, 1)],
                                         pair(D), ALU.mult, ALU.add).then_inc(s_yev, 1)
            barrier(eng, "qkv")
            eng.wait_ge(s_st, 1)
            dve(eng, eng.tensor_copy(st_out[:, :, :, :].rearrange("p c a n -> p (c a n)"), ps[:, 6, :]))
            dve(eng, eng.tensor_copy(stp_out[:, :, :].rearrange("p c n -> p (c n)"), ps[0:STILES, 7, 0:2 * P]))
            eng.sem_inc(s_stc, 1)
            barrier(eng, "states")
            eng.wait_ge(s_causal, 2)
            with eng.Fori(0, HEADS) as h:
                for n, b in enumerate(ORDER):
                    eng.wait_ge(s_bias, h * QB + (n + 2))
                    eng.tensor_tensor(prob[:, off[b] + b * P:off[b + 1]], prob[:, off[b] + b * P:off[b + 1]],
                                      causal[:, :], ALU.add).then_inc(s_bm, 1)
                eng.wait_ge(s_qk, h + 2)
                for n, b in enumerate(ORDER):
                    p = prob[:, off[b]:off[b + 1]]
                    eng.wait_ge(s_bm, h * QB + (n + 2))
                    eng.scalar_tensor_tensor(p, ps[:, b, 0:(b + 1) * P], SCALE, p, ALU.mult, ALU.add)\
                       .then_inc(s_sc, 1)
                    eng.wait_ge(s_sc, h * QB + (n + 2))
                    eng.tensor_reduce(stat[:, 2, b:b + 1], p, AX_X, ALU.max).then_inc(s_mx, 1)
                    eng.wait_ge(s_mx, h * QB + (n + 2))
                    eng.tensor_scalar(stat[:, 0, b:b + 1], stat[:, 2, b:b + 1], -1.0, None, ALU.mult)\
                       .then_inc(s_nm, 1)
                for n, b in enumerate(ORDER):
                    p = prob[:, off[b]:off[b + 1]]
                    eng.wait_ge(s_ex, h * QB + (n + 2))
                    eng.reciprocal(stat[:, 2, b:b + 1], stat[:, 1, b:b + 1]).then_inc(s_rs2, 1)
                    eng.wait_ge(s_rs2, h * QB + (n + 2))
                    eng.tensor_scalar(p, p, stat[:, 2, b:b + 1], None, ALU.mult).then_inc(s_pr, 1)
                for n, (a, b2, bank) in enumerate(((2, 4, 5), (1, 2, 4), (0, 1, 7))):
                    eng.wait_ge(s_pt, h * 3 + n + 2)
                    eng.wait_ge(s_pv, h + 1)
                    eng.tensor_copy(prob_t[:, poff[a]:poff[b2]], ps[:, bank, 0:poff[b2] - poff[a]])\
                       .then_inc(s_ptc, 1)
            barrier(eng, "prompt")
            dve(eng, eng.tensor_scalar(qs[:, :, :], q[:, :, SEQ:T], SCALE, None, ALU.mult))
            dve(eng, eng.tensor_copy(ks[:, :, :], k[:, :, SEQ:T]))
            dve(eng, eng.tensor_reduce(head_of[:, :], ident[:, :].rearrange("p (a h) -> p h a", h=HEADS), AX_X, ALU.add))
            for g in range(2):
                dve(eng, eng.tensor_copy(sel[:, g, :, :], head_of[:, GH * g:GH * g + GH].rearrange(
                    "p (j o) -> p j o", o=1).to_broadcast([P, GH, NS])))
                mul(sel_c[:, g, :, :], sel[0:HEADS, g, :, :], cum[:, SEQ:T].rearrange(
                    "p (o t) -> p o t", o=1).to_broadcast([HEADS, GH, NS]))
            dve(eng, eng.tensor_scalar(neg_c[:, :], cum[:, SEQ:T], -1.0, None, ALU.mult))
            dve(eng, eng.tensor_copy(rep[:, :, :], ident[0:NS, 0:NS].rearrange("p (o t) -> p o t", o=1)
                                     .to_broadcast([NS, GH, NS])))
            dve(eng, eng.memset(s_tot[:, :], 0.0))
            eng.wait_ge(s_lft2, 1)
            for c in range(2):
                dve(eng, eng.tensor_copy(lf_past[:, :, :, 4 * c:4 * c + 4].rearrange("k b p h -> k (b p) h"),
                                         ps[:, c, :].rearrange("k (h r) -> k r h", h=4)))
            dve(eng, eng.memset(lf_later[:, :, N_PAGES - 1, :], 0.0))
            for p in range(N_PAGES - 2, -1, -1):
                add(lf_later[:, :, p, :], lf_later[:, :, p + 1, :], lf_past[:, :, p + 1, :])
            eng.sem_inc(s_sp, 1)
            eng.wait_ge(s_spe, 1)
            dve(eng, eng.tensor_copy(decay[:, :, :].rearrange("p b k -> p (b k)"), ps[:, 0:2, :].rearrange("p a n -> p (a n)")))
            dve(eng, eng.tensor_copy(mask[:, :], ps[:, 6, 0:NS + DEC_BATCH]))
            dve(eng, eng.tensor_copy(c_query[:, :], ps[:, 6, 64:66]))
            for g in range(2):
                dve(eng, eng.scalar_tensor_tensor(new_sc[:, g, :], ps[:, 6, 128 + NS * g:128 + NS * (g + 1)],
                                                  c_query[:, g:g + 1], mask[:, 0:NS], ALU.add, ALU.add))
                dve(eng, eng.tensor_reduce(run_max[:, g, GROUPS:GROUPS + 1], new_sc[:, g, :], AX_X, ALU.max))
            eng.sem_inc(s_spc, 1)
            with eng.Fori(0, DEC_BATCH) as b:
                def turned(r, dst):
                    eng.wait_ge(s_tt, b * ROUNDS + (r + 1 + 1))
                    eng.tensor_copy(dst, ps[:, 2 * (r % 2) + 1, :]).then_inc(s_tcd, 1)

                def copy_scores(pr):
                    eng.wait_ge(s_sco, b * N_PAGES + 2 * (pr + 1) + 1)
                    for g in range(2):
                        ins = eng.tensor_scalar(scores[:, g, pr * 256:(pr + 1) * 256], ps[:, 5, 256 * g:256 * g + 256],
                                                c_query[:, g:g + 1], None, ALU.add)
                    ins.then_inc(s_td, 1)

                def group_max(gr):
                    eng.wait_ge(s_td, b * (N_PAGES // 4) + (gr + 2))
                    eng.wait_ge(s_ta, b * (N_PAGES // 4) + (gr + 2))
                    eng.tensor_reduce(run_max[:, :, gr:gr + 1].rearrange("p g o -> p (g o)"),
                                      scores[:, :, gr * 512:(gr + 1) * 512], AX_X, ALU.max).then_inc(s_sm, 1)

                for p in range(N_PAGES):
                    eng.wait_ge(s_sco, b * N_PAGES + (max(p - 1, 0) + 1))
                    turned(p, key_t[:, p % 2, 1, :])
                    if p % 4 == 1 and p > 1:
                        copy_scores(p // 2 - 1)
                        group_max(p // 4 - 1)
                copy_scores(N_PAGES // 2 - 1)
                group_max(GROUPS - 1)
                eng.wait_ge(s_sm, b * 9 + (GROUPS + 1))
                eng.tensor_reduce(s_max[:, :], run_max[:, :, :], AX_X, ALU.max).then_inc(s_sm, 1)
                eng.wait_ge(s_sm, b * 9 + (GROUPS + 2))
                eng.tensor_scalar(s_nmax[:, :], s_max[:, :], -1.0, mask[:, bass.ds(b + NS, 1)], ALU.mult, ALU.add)\
                   .then_inc(s_sm, 1)
                for gr in range(GROUPS):
                    eng.wait_ge(s_pvp, b * N_PAGES + (N_PAGES + 4 * max(gr - 1, 0) + 1))
                    turned(N_PAGES + gr, prob_st[:, gr % 2, 1, :])
                eng.wait_ge(s_sx, b * 5 + 6)
                eng.tensor_tensor(new_pr[:, :, :], new_pr[:, :, :], new_ex[:, :, :], ALU.add).then_inc(s_sm, 1)
                eng.tensor_reduce(part_sum[:, :], exp_part[:, :, :], AX_X, ALU.add).then_inc(s_sm, 1)
                eng.wait_ge(s_sm, b * 9 + 9)
                eng.tensor_tensor(s_tot[:, :], s_tot[:, :], part_sum[:, :], ALU.add).then_inc(s_sm, 1)
            eng.wait_ge(s_sm, 9 * DEC_BATCH + 1)
            dve(eng, eng.reciprocal(s_rec1[:, :], s_tot[:, :]))
            eng.wait_ge(s_fin, 1)
            eng.tensor_copy(new_pt[:, :, :].rearrange("p g n -> p (g n)"), ps[0:NS, 6, 0:2 * P]).then_inc(s_finc, 1)
            eng.wait_ge(s_fin, 2)
            for g in range(2):
                ins = eng.tensor_scalar(o_rows[:, g, :], ps[:, 7, g * P:(g + 1) * P], s_rec1[:, g:g + 1], None, ALU.mult)
            ins.then_inc(s_finc, 1)
            eng.wait_ge(s_fin, 3)
            eng.tensor_copy(q[:, :, SEQ:T], ps[:, 6, 0:2 * P].rearrange("p (h t) -> p h t", t=NS)).then_inc(s_finc, 1)
            barrier(eng, "sample")
            for t in range(1, KH, 2):
                eng.wait_ge(s_y1h, t + 1)
                eng.tensor_tensor(y1_lo[:, t, :], u[:, t, :], y1_hi[:, t, :].bitcast(F32), ALU.subtract)\
                   .then_inc(s_y1l2, 1)
            with eng.Fori(0, ph_glu.times) as i:
                for j in range(4):
                    eng.wait_ge(s_gg, i * 4 + j + 2)
                    t = u[:, bass.ds(i * 4 + j, 1), :].rearrange("p a n -> p (a n)")
                    eng.tensor_tensor(t, t, glu_gate[:, j % 2, :], ALU.mult).then_inc(s_ys, 1)
            eng.wait_ge(s_used, ph_glu.used(ph_glu.times - 1, 3))
            for src, hi, lo, s_h1, s_l1 in ((u, ys_hi, ys_lo, s_ysh, s_ysl), (q, ya_hi, ya_lo, s_yah, s_yal)):
                for t in range(KH):
                    if hi is ys_hi:
                        eng.wait_ge(s_ys, t + 2)
                    eng.tensor_copy(hi[:, t, :], src[:, t, :]).then_inc(s_h1, 1)
                for t in range(KH):
                    eng.wait_ge(s_h1, t + 1)
                    eng.tensor_tensor(lo[:, t, :], src[:, t, :], hi[:, t, :].bitcast(F32), ALU.subtract)\
                       .then_inc(s_l1, 1)
            with eng.Fori(0, ph_merge.times) as i:
                mt = tile_of(merged, i)
                eng.wait_ge(s_gs, i + 2)
                eng.wait_ge(s_used, ph_merge.used(i, 4))
                eng.tensor_tensor(two(mt), two(mt), pair(C), ALU.mult).then_inc(s_mg, 1)
                eng.wait_ge(s_ga, i + 2)
                eng.wait_ge(s_used, ph_merge.used(i, 5))
                eng.tensor_tensor(two(att_gate[:, :]), two(att_gate[:, :]), pair(D), ALU.mult).then_inc(s_mg, 1)
                eng.wait_ge(s_mg, i * 3 + 3)
                eng.tensor_tensor(mt, mt, att_gate[:, :], ALU.add).then_inc(s_mg, 1)
            barrier(eng, "merged")
            for t in range(1, KD, 2):
                eng.tensor_copy(xn_hi[:, t, :], merged[:, t, :]).then_inc(s_mhi2, 1)
            for t in range(1, KD, 2):
                eng.wait_ge(s_mhi2, t // 2 + 1)
                eng.tensor_tensor(xn_lo[:, t, :], merged[:, t, :], xn_hi[:, t, :].bitcast(F32), ALU.subtract)\
                   .then_inc(s_mlo2, 1)
            eng.wait_ge(s_x2c, 17)
            with eng.Fori(0, ph_out.times) as i:
                for c in range(2):
                    t = x_t[:, bass.ds(i * 2 + c, 1), :].rearrange("p a n -> p (a n)")
                    eng.wait_ge(s_used, ph_out.used(i, 2 * c + 1))
                    eng.tensor_tensor(two(t), two(t), pair(c), ALU.add).then_inc(s_res[c], 1)
            barrier(eng, "out")
            norm_dve(eng, "ffn")
            barrier(eng, "ffn_normed")
            with eng.Fori(0, FF_BLOCKS) as n:
                up, down = (p.in_block(n) for p in ph_ffn)
                with eng.Fori(0, up.times) as i:
                    eng.wait_ge(s_silu, n * FF_TILES + i + 2)
                    eng.wait_ge(s_used, up.used(i, 3))
                    eng.wait_ge(s_hl, n * FF_TILES + i + 1)
                    eng.tensor_tensor(two(hid[:, :]), two(ff_act[:, :]), pair(B), ALU.mult).then_inc(s_hid, 1)
                with eng.Fori(0, down.times) as i:
                    for c in range(2):
                        t = x_t[:, bass.ds(i * 2 + c, 1), :].rearrange("p a n -> p (a n)")
                        eng.wait_ge(s_used, down.used(i, 2 * c + 1))
                        eng.tensor_tensor(two(t), two(t), pair(C + c), ALU.add).then_inc(s_dn[c], 1)
            barrier(eng, "ffn")
            for t in range(4):
                for g in range(2):
                    eng.wait_ge(s_yt, 4 * t + 2 * g + 2)
                    if t >= 2:
                        eng.wait_ge(s_yst[t % 2], 16)
                    eng.tensor_copy(y_nat[:, t % 2, (2 * g + 1) * 512:(2 * g + 2) * 512], ps[:, 4 * (t % 2) + 2 * g + 1, :])\
                       .then_inc(s_ycd, 1)
            eng.wait_ge(s_yt, 20)
            eng.wait_ge(s_yst[0], 32)
            eng.tensor_copy(y_nat[0:NS, 0, :].rearrange("p (g n) -> p g n", n=512), ps[0:NS, 0:4, :]).then_inc(s_ycd, 1)

        @block.tensor
        def _(pe):
            pe.sem_inc(s_used, RAW)
            pe.wait_ge(s_ident, 3)
            pe.wait_ge(s_vec, 96)
            pe.transpose(ps[:, 0, 0:50], rows[:, :], ident[0:50, 0:50]).then_inc(s_setup_t, 1)
            for t in range(4):
                if t == 1:
                    pe.wait_ge(s_setup_c, 1)
                pe.wait_ge(s_x[t % 2], 16 * (t // 2 + 1))
                for g in range(4):
                    if t >= 2:
                        pe.wait_ge(s_xc, 4 * (t - 2) + g + 1)
                    for c in range(4):
                        mm = pe.transpose(ps[:, g if t % 2 else 4 + g, c * P:(c + 1) * P],
                                          x_nat[:, t % 2, (4 * g + c) * P:(4 * g + c + 1) * P], ident[:, :])
                    mm.then_inc(s_xt, 1)
            pe.wait_ge(s_xs, 16)
            pe.wait_ge(s_xc, 9)
            for c in range(KD):
                mm = pe.transpose(ps[:, 4, c * NS:(c + 1) * NS], x_smp[:, c * P:(c + 1) * P], ident[0:NS, 0:NS])
            mm.then_inc(s_xt, 1)
            barrier(pe, "setup")
            norm_pe(pe, "mix")
            pe.drain().then_inc(s_all, 1)
            xh = lambda k0: halves(xn_hi, lambda kt: k0 + kt)
            xl = lambda k0: halves(xn_lo, lambda kt: k0 + kt)
            for j in range(2):
                normed_tiles(pe, "mix", KU * (j + 1))
                ph_f.product(pe, 0, j, C, xh(KU * j), xl(KU * j), j == 0, j == 1)
            pe.drain().then_inc(s_fm, 1)

            def u_tiles(lo, hi):
                with pe.Fori(lo, hi) as i:
                    for j in range(4):
                        if j % 2 == 0:
                            pe.wait_ge(s_uev[j // 2], i + 1)
                        ph_u.product(pe, i, j, j // 2, xh(KU * (j % 2)), xl(KU * (j % 2)), j % 2 == 0, j % 2 == 1)

            u_tiles(0, 2)
            pe.wait_ge(s_small, 16 * 6)
            pe.wait_ge(s_dve_s, 2)
            for n, r in enumerate((N_ABR, N_ABI, N_FR, N_FI)):
                pe.transpose(ps[:, 6, 64 + 32 * n:96 + 32 * n], nt(r), ident[0:STILES, 0:STILES])
            for c in range(2):
                for a in range(2):
                    mm = pe.transpose(ps[:, 7, 256 * c + P * a:256 * c + P * a + P], h0_nat[:, c, a, :], ident[:, :])
            mm.then_inc(s_setup_t, 1)
            u_tiles(2, 4)
            pe.wait_ge(s_dve_s, 3)
            n = 0
            for w in (b_pad, c_pad):
                for c in range(2):
                    for half in range(2):
                        n += 1
                        if n > 4:
                            pe.wait_ge(s_setup_c, n - 3)
                        for t in range(4):
                            tile = w[:, c, 4 * half + t]
                            mm = pe.transpose(ps[:, 4 + n % 4, t * P:(t + 1) * P],
                                              tile.rearrange("p j g c -> p (j g c)") if w is b_pad
                                              else tile.rearrange("p g c -> p (g c)"), ident[:, :])
                        mm.then_inc(s_setup_t, 1)
            pe.wait_ge(s_lf, 1)
            pe.wait_ge(s_setup_c, 9)
            for blk in range(5):
                n = P if blk < 4 else NS
                for c, t in enumerate((lf_w[:, 0, :], cum[:, :])):
                    mm = pe.transpose(ps[0:n, 7, 16 * blk + 8 * c:16 * blk + 8 * c + 8],
                                      t[:, blk * P:blk * P + n], ident[0:HEADS, 0:HEADS])
            mm.then_inc(s_lft, 1)
            barrier(pe, "u")

            def b_product(i, n):
                j, c = n // 2, n % 2
                r = slice(32 * j, 32 * j + 32)
                pe.wait_ge(s_buc, i * 8 + n + 1)
                for half in range(2):
                    mm = pe.matmul(ps[:, 2 * C + half, 0:HT], use_b[r, c, :],
                                   use_u[r, half * HT:(half + 1) * HT], start=True, stop=True)
                mm.then_inc(s_bu, 1)

            def c_product(i, j):
                pe.wait_ge(s_h, i * 4 + j + 2)
                pe.wait_ge(s_hs, i * 4 + j + 2)
                for c, h in enumerate((h_re, h_im)):
                    for half in range(2):
                        mm = pe.matmul(ps[32 * j:32 * j + 32, 2 * D + half, 0:HT], use_c[:, c, 32 * j:32 * j + 32],
                                       h[:, j % 2, half * HT:(half + 1) * HT], start=c == 0, stop=c == 1)
                mm.then_inc(s_ch, 1)

            def square_sum(i, n):
                pe.wait_ge(s_ev, i * 3 + n + 2)
                for half in range(2):
                    mm = pe.matmul(ps[:, 2 * C + half, 0:HT], ones[:, :],
                                   v[:, bass.ds(i, 1), half * HT:(half + 1) * HT].rearrange("p a n -> p (a n)"),
                                   start=True, stop=True)
                mm.then_inc(s_qsum, 1)

            def part(i, j, quarter, pair):
                ph_qkv.product(pe, i, j, pair, xh(KU * (j % 2)), xl(KU * (j % 2)), j % 2 == 0, j % 2 == 1,
                               tiles=range(4 * quarter, 4 * quarter + 4), wait=quarter == 0, done=quarter == 1)
                if j % 2 and quarter:
                    pe.drain().then_inc(s_m, 1)

            with pe.Fori(0, HEADS) as i:
                pe.wait_ge(s_ub, i * 2 + 3)
                b_product(i, 0)
                pe.wait_ge(s_ev, i * 3 + 1)
                part(i, 0, 0, A)
                b_product(i, 1)
                part(i, 0, 1, A)
                b_product(i, 2)
                part(i, 1, 0, A)
                b_product(i, 3)
                part(i, 1, 1, A)
                part(i, 2, 0, B)
                part(i, 2, 1, B)
                pe.wait_ge(s_uc, i + 2)
                pe.wait_ge(s_yev, i + 1)
                c_product(i, 0)
                b_product(i, 4)
                part(i, 3, 0, B)
                pe.wait_ge(s_buc, i * 8 + 6)
                square_sum(i, 0)
                part(i, 3, 1, B)
                pe.wait_ge(s_qrs, i * 2 + 2)
                b_product(i, 5)
                part(i, 4, 0, A)
                c_product(i, 1)
                b_product(i, 6)
                part(i, 4, 1, A)
                pe.wait_ge(s_buc, i * 8 + 8)
                square_sum(i, 1)
                part(i, 5, 0, A)
                pe.wait_ge(s_qrs, i * 2 + 3)
                b_product(i, 7)
                part(i, 5, 1, A)
                c_product(i, 2)
                c_product(i, 3)
            barrier(pe, "qkv")
            for c in range(2):
                for a in range(2):
                    pe.transpose(ps[:, 6, (2 * c + a) * P:(2 * c + a + 1) * P],
                                 st_s[:, c, 4 * a:4 * a + 4, :].rearrange("p b s -> p (b s)"), ident[:, :])
                mm = pe.transpose(ps[0:STILES, 7, c * P:(c + 1) * P], st_p[:, c, :], ident[:, :])
            mm.then_inc(s_st, 1)
            barrier(pe, "states")

            def prompt_head(i, e):
                h = i * 2 + e
                s = stage[:, e]
                pe.wait_ge(s_cm, h + 2)
                pe.wait_ge(s_ptc, h * 3 + 1)
                pe.matmul(ps[:, 7, :], ones[0:HEADS, :], cm[:, 0:SEQ], start=True, stop=True).then_inc(s_cb, 1)
                pe.wait_ge(s_stage, h * 3 + 4)
                pe.wait_ge(s_sc, h * QB + 1)
                for b in range(QB):
                    mm = pe.matmul(ps[:, b, 0:(b + 1) * P], s[:, 0, b * P:(b + 1) * P],
                                   s[:, 1, 0:(b + 1) * P], start=True, stop=True)
                mm.then_inc(s_qk, 1)
                pe.wait_ge(s_oc, h + 1)
                for c in range(2):
                    for b in range(QB):
                        pe.transpose(ps[:, 4 + c, b * P:(b + 1) * P], s[:, 1 + c, b * P:(b + 1) * P], ident[:, :])
                    mm = pe.transpose(ps[0:NS, 6, c * P:(c + 1) * P], s[:, 1 + c, SEQ:T], ident[:, :])
                mm.then_inc(s_kv, 1)
                pe.wait_ge(s_kvc, h + 2)
                for n, b in enumerate(ORDER):
                    pe.wait_ge(s_pr, h * QB + (n + 2))
                    for kb, bank in ((0, 7), (1, 4), (2, 5), (3, 5))[:b + 1]:
                        c = (b - kb + (2 if kb == 3 else 0)) * P
                        mm = pe.transpose(ps[:, bank, c:c + P], prob[:, off[b] + kb * P:off[b] + (kb + 1) * P],
                                          ident[:, :])
                    if n:
                        mm.then_inc(s_pt, 1)
                for n, kb in enumerate((2, 3, 1, 0)):
                    pe.wait_ge(s_ptc, h * 3 + (max(n, 1) + 1))
                    mm = pe.matmul(ps[:, 6, kb * P:SEQ], nat_kv[:, 1, kb, :], prob_t[:, poff[kb]:poff[kb + 1]],
                                   start=n == 0, stop=kb == 0, skip_group_check=True)
                mm.then_inc(s_pv, 1)

            with pe.Fori(0, HEADS // 2) as i:
                prompt_head(i, 0)
                prompt_head(i, 1)
            barrier(pe, "prompt")
            pe.wait_ge(s_lfp, 16 * DEC_BATCH * N_PAGES)
            for h in range(HEADS):
                mm = pe.transpose(ps[:, h // 4, (h % 4) * P:(h % 4 + 1) * P], lf_rows[:, :, h], ident[:, :])
            mm.then_inc(s_lft2, 1)
            pe.wait_ge(s_sp, 1)
            pe.wait_ge(s_pool_c, 4)
            for b in range(DEC_BATCH):
                out = ps[:, b // 4, (b % 4) * PAGE:(b % 4 + 1) * PAGE]
                pe.matmul(out, lf_past[:, b, :, :].rearrange("k p h -> k (p h)"), later[:, :], start=True, stop=False)
                pe.matmul(out, lf_later[:, b, :, :].rearrange("k p h -> k (p h)"), ones[:, :], start=False, stop=True)
            flat = "p j t -> p (j t)"
            pe.matmul(ps[:, 6, 0:NS + DEC_BATCH], rep[:, :, :].rearrange(flat), mask32[:, :], start=True, stop=True)
            for g in range(2):
                pe.matmul(ps[:, 6, 64 + g:65 + g], sel_c[:, g, :, :].rearrange(flat), ones[0:HEADS, 0:1],
                          start=True, stop=True)
                new = slice(128 + NS * g, 128 + NS * (g + 1))
                pe.matmul(ps[:, 6, new], sel[0:HEADS, g, :, :].rearrange(flat), neg_c[:, :], start=True, stop=False,
                          skip_group_check=True)
                for j in range(GH):
                    pe.matmul(ps[32 * j:32 * j + 32, 6, new], qs[:, GH * g + j, :], ks[:, GH * g + j, :],
                              start=False, stop=True, skip_group_check=True)
            pe.matmul(ps[:, 7, 0:2 * P], ident[:, :], zeros[:, :], start=True, stop=False,
                      skip_group_check=True).then_inc(s_spe, 1)
            pe.sem_inc(s_pvp, N_PAGES)
            pe.wait_ge(s_spc, 1)
            with pe.Fori(0, DEC_BATCH) as b:
                def banks_free(r):
                    pe.wait_ge(s_tca, b * ROUNDS + (max(r - 1, 0) + 1))
                    pe.wait_ge(s_tcd, b * ROUNDS + (max(r - 1, 0) + 1))

                def turned_copied(r):
                    pe.wait_ge(s_tca, b * ROUNDS + (r + 1 + 1))
                    pe.wait_ge(s_tcd, b * ROUNDS + (r + 1 + 1))

                def turn_page(p):
                    pe.wait_ge(s_page[p % PG], b * 64 + 16 * (p // PG + 1))
                    banks_free(p)
                    for h in range(HEADS):
                        mm = pe.transpose(ps[:, 2 * (p % 2) + h // GH, (h % GH) * PAGE:(h % GH + 1) * PAGE],
                                          page[:, p % PG, h * P:(h + 1) * P], ident[:, :])
                    mm.then_inc(s_tt, 1)

                def score(p):
                    turned_copied(p)
                    if p % 2 == 0:
                        pe.wait_ge(s_td if p // 2 % 2 else s_ta, b * (N_PAGES // 4) + p // 4 + 1)
                        pe.wait_ge(s_dp, b * (N_PAGES // 2) + (p // 2 + 1 + 1))
                        for g in range(2):
                            pe.matmul(ps[:, 4 + p // 2 % 2, 256 * g:256 * g + 256], sel[:, g, :, :].rearrange(flat),
                                      decay_p[:, p // 2 % 4, :, :].rearrange("p e n -> p (e n)"),
                                      start=g == 0, stop=False, skip_group_check=True)
                    for g in range(2):
                        cols = slice(256 * g + PAGE * (p % 2), 256 * g + PAGE * (p % 2) + PAGE)
                        bank = 4 + p // 2 % 2
                        for j in range(GH):
                            mm = pe.matmul(ps[32 * j:32 * j + 32, bank, cols], qs[:, GH * g + j, :],
                                           key_t[:, p % 2, g, j * PAGE:(j + 1) * PAGE], start=False, stop=True,
                                           skip_group_check=True)
                    mm.then_inc(s_sco, 1)

                def turn_prob(gr):
                    pe.wait_ge(s_sx, b * 5 + (gr + 2))
                    banks_free(N_PAGES + gr)
                    for g in range(2):
                        for p in range(4):
                            mm = pe.transpose(ps[:, 2 * (gr % 2) + g, p * PAGE:(p + 1) * PAGE],
                                              scores[:, g, (4 * gr + p) * PAGE:(4 * gr + p + 1) * PAGE], ident[:, :])
                    mm.then_inc(s_tt, 1)

                def sum_values(gr):
                    turned_copied(N_PAGES + gr)
                    for p in range(4 * gr, 4 * gr + 4):
                        pe.wait_ge(s_page[p % PG], b * 64 + 16 * (2 + p // PG + 1))
                        for h in range(HEADS):
                            g, j = h // GH, h % GH
                            mm = pe.matmul(ps[32 * j:32 * j + 32, 7, g * P:(g + 1) * P],
                                           prob_st[:, gr % 2, g, (p % 4) * PAGE + 32 * j:(p % 4) * PAGE + 32 * j + 32],
                                           page[:, p % PG, h * P:(h + 1) * P], start=False, stop=False,
                                           skip_group_check=True)
                        mm.then_inc(s_pvp, 1)

                turn_page(0)
                for p in range(1, N_PAGES):
                    turn_page(p)
                    score(p - 1)
                score(N_PAGES - 1)
                turn_prob(0)
                for gr in range(1, GROUPS):
                    turn_prob(gr)
                    sum_values(gr - 1)
                sum_values(GROUPS - 1)
            pe.wait_ge(s_sm, 9 * DEC_BATCH + 1)
            for g in range(2):
                mm = pe.transpose(ps[0:NS, 6, g * P:(g + 1) * P], new_pr[:, g, :], ident[:, :])
            mm.then_inc(s_fin, 1)
            pe.wait_ge(s_finc, 1)
            for h in range(HEADS):
                g, j = h // GH, h % GH
                mm = pe.matmul(ps[32 * j:32 * j + 32, 7, g * P:(g + 1) * P], new_pt[:, g, 32 * j:32 * j + 32],
                               vs_nat[:, h, :], start=False, stop=True, skip_group_check=True)
            mm.then_inc(s_fin, 1)
            pe.wait_ge(s_finc, 2)
            for g in range(2):
                mm = pe.transpose(ps[:, 6, g * P:(g + 1) * P], o_rows[:, g, :], ident[:, :])
            mm.then_inc(s_fin, 1)
            barrier(pe, "sample")
            y1h, y1l = halves(y1_hi, lambda kt: kt), halves(y1_lo, lambda kt: kt)
            pe.wait_ge(s_y1l, KH // 2)
            pe.wait_ge(s_y1l2, KH // 2)
            with pe.Fori(0, ph_glu.times) as i:
                for j in range(4):
                    pe.wait_ge(s_gg, i * 4 + 1)
                    ph_glu.product(pe, i, j, j, y1h, y1l, True, True)
            pe.wait_ge(s_gg, 9)
            ysh, ysl = halves(ys_hi, lambda kt: kt), halves(ys_lo, lambda kt: kt)
            yah, yal = halves(ya_hi, lambda kt: kt), halves(ya_lo, lambda kt: kt)
            with pe.Fori(0, ph_merge.times) as i:
                pe.wait_ge(s_gs, i + 1)
                ph_merge.product(pe, i, 0, A, xh(0), xl(0), True, False)
                ph_merge.product(pe, i, 1, A, xh(KU), xl(KU), False, True)
                pe.wait_ge(s_ga, i + 1)
                ph_merge.product(pe, i, 2, B, xh(0), xl(0), True, False)
                ph_merge.product(pe, i, 3, B, xh(KU), xl(KU), False, True)
                pe.wait_ge(s_mg, i * 3 + 1)
                pe.wait_ge(s_ysl, KH)
                ph_merge.product(pe, i, 4, C, ysh, ysl, True, True)
                pe.wait_ge(s_yal, KH)
                ph_merge.product(pe, i, 5, D, yah, yal, True, True)
            barrier(pe, "merged")
            for t in range(4):
                pe.wait_ge(s_x2[t % 2], 16 * (t // 2 + 1))
                for g in range(4):
                    if t >= 2:
                        pe.wait_ge(s_x2c, 4 * (t - 2) + g + 1)
                    for c in range(4):
                        mm = pe.transpose(ps[:, g if t % 2 else 4 + g, c * P:(c + 1) * P],
                                          x_again[:, t % 2, (4 * g + c) * P:(4 * g + c + 1) * P], ident[:, :])
                    mm.then_inc(s_x2t, 1)
            pe.wait_ge(s_xs2, 16)
            pe.wait_ge(s_x2c, 9)
            for c in range(KD):
                mm = pe.transpose(ps[:, 4, c * NS:(c + 1) * NS], x_smp2[:, c * P:(c + 1) * P], ident[0:NS, 0:NS])
            mm.then_inc(s_x2t, 1)
            pe.wait_ge(s_x2c, 16)
            for s in (s_mhi, s_mhi2, s_mlo, s_mlo2):
                pe.wait_ge(s, KD // 2)
            with pe.Fori(0, ph_out.times) as i:
                for j in range(4):
                    if j % 2 == 0:
                        pe.wait_ge(s_res[j // 2], i + 1)
                    ph_out.product(pe, i, j, j // 2, xh(KU * (j % 2)), xl(KU * (j % 2)), j % 2 == 0, j % 2 == 1)
            barrier(pe, "out")
            norm_pe(pe, "ffn")
            pe.drain().then_inc(s_all, 1)
            with pe.Fori(0, FF_BLOCKS) as n:
                up, down = (p.in_block(n) for p in ph_ffn)
                with pe.Fori(0, up.times) as i:
                    pe.wait_ge(s_silu, n * FF_TILES + i + 1)
                    normed_tiles(pe, "ffn", KU)
                    up.product(pe, i, 0, A, xh(0), xl(0), True, False)
                    normed_tiles(pe, "ffn", KD)
                    up.product(pe, i, 1, A, xh(KU), xl(KU), False, True)
                    pe.wait_ge(s_hid, n * FF_TILES + i + 1)
                    up.product(pe, i, 2, B, xh(0), xl(0), True, False)
                    up.product(pe, i, 3, B, xh(KU), xl(KU), False, True)
                with pe.Fori(0, down.times) as i:
                    for c in range(2):
                        pe.wait_ge(s_dn[c], n * (KD // 2) + i + 1)
                        for j, (k0, nk) in enumerate(FF_UNITS):
                            pe.wait_ge(s_hl, n * FF_TILES + (k0 + nk + 1))
                            down.product(pe, i, 2 * c + j, C + c, halves(hid_hi, lambda kt: k0 + kt),
                                         halves(hid_lo, lambda kt: k0 + kt), j == 0, j == 1, n=nk)
            barrier(pe, "ffn")
            for t in range(5):
                n = P if t < 4 else NS
                if t >= 2:
                    pe.wait_ge(s_yca, 2 * (t - 1))
                    pe.wait_ge(s_ycd, 2 * (t - 1))
                for g in range(4):
                    for c in range(4):
                        mm = pe.transpose(ps[0:n, 4 * (t % 2) + g, c * P:(c + 1) * P],
                                          x_t[:, 4 * g + c, t * P:t * P + n], ident[:, :])
                    mm.then_inc(s_yt, 1)


_INS = ['x_prompt', 'x_sample', 'cache_k', 'cache_v', 'cache_logf', 'state_ssm_re', 'state_ssm_im', 'page_table',
        'norm_mix_g', 'w_in', 'b_f', 'q_norm_g', 'k_norm_g', 'ssm_a_re', 'ssm_a_im', 'ssm_log_dt', 'ssm_b_re',
        'ssm_b_im', 'ssm_c_re', 'ssm_c_im', 'ssm_d', 'w_glu', 'b_glu', 'w_br_ssm', 'w_br_att', 'w_out',
        'norm_ffn_g', 'w_ffn_gate', 'w_ffn_up', 'w_ffn_down']
_OUTS = [(1, 512, 2048), (8, 4, 2048), (1, 1, 512, 8, 128), (1, 1, 512, 8, 128), (1, 1, 512, 8), (1, 1, 64, 64),
         (1, 1, 64, 64), (1, 8, 4, 8, 128), (1, 8, 4, 8, 128), (1, 8, 4, 8), (1, 8, 64, 64), (1, 8, 64, 64)]


def kernel(**inputs):
    import numpy as _np
    import concourse.bacc as _bacc
    from concourse import mybir as _mybir
    from concourse.bass_utils import run_bass_kernel_spmd as _run

    nc = _bacc.Bacc("TRN2", target_bir_lowering=False, num_devices=1)
    arrays, args = {}, []
    for name in _INS:
        a = _np.ascontiguousarray(inputs[name])
        arrays[f"in_{name}_dram"] = a
        args.append(nc.dram_tensor(f"in_{name}_dram", a.shape, _mybir.dt.from_np(a.dtype), kind="ExternalInput").ap())
    for i, shape in enumerate(_OUTS):
        args.append(nc.dram_tensor(f"out_{i}_dram", shape, _mybir.dt.float32, kind="ExternalOutput").ap())
    build(nc, *args)
    r = _run(nc, [arrays], core_ids=[0])
    return tuple(r.results[0][f"out_{i}_dram"] for i in range(len(_OUTS)))
```
